# Optimizing a Trainium2 kernel written in Bass

```python
import math
import jax
import jax.numpy as jnp
from jax import lax
import numpy as np

D_MODEL = 1024
BATCH = 1
SEQ = 256
DEPTH = 1

SSD_EXPAND = 2
SSD_D_INNER = SSD_EXPAND * D_MODEL
SSD_HEAD_DIM = 64
SSD_HEADS = SSD_D_INNER // SSD_HEAD_DIM
SSD_GROUPS = 8
SSD_HEADS_PER_GROUP = SSD_HEADS // SSD_GROUPS
SSD_STATE = 128
SSD_CONV = 5
SSD_CHUNK = 128
SSD_CONV_DIM = SSD_D_INNER + 2 * SSD_GROUPS * SSD_STATE
SSD_NORM_EPS = 1e-5

POOL_WIDTH = D_MODEL
POOL_WINDOWS = (2, 4, 8, 16)
POOL_GROUPS = len(POOL_WINDOWS)
POOL_GROUP_DIM = POOL_WIDTH // POOL_GROUPS

N_BRANCHES = 2
IN_PROJ_SIZES = (SSD_D_INNER, SSD_CONV_DIM, SSD_HEADS, SSD_HEADS, POOL_WIDTH, N_BRANCHES * D_MODEL)
IN_PROJ_DIM = sum(IN_PROJ_SIZES)

MOE_GROUPS = 4
MOE_EXPERTS_PER_GROUP = 8
MOE_EXPERTS = MOE_GROUPS * MOE_EXPERTS_PER_GROUP
MOE_TOP_K = 2
MOE_HIDDEN = 512

DEEPNORM_ALPHA = (2.0 * DEPTH) ** 0.25
DEEPNORM_BETA = (8.0 * DEPTH) ** -0.25
LN_EPS = 1e-5
N_ADA = 6

kernel_name = 'hybrid_bissd_multipool_hmoe_block'

def _layernorm(x):
    xf = x.astype(jnp.float32)
    mu = jnp.mean(xf, axis=-1, keepdims=True)
    var = jnp.mean(jnp.square(xf - mu), axis=-1, keepdims=True)
    return ((xf - mu) * lax.rsqrt(var + LN_EPS)).astype(x.dtype)

def _modulate(x, shift, scale):
    return _layernorm(x) * (1.0 + scale[:, None, :]) + shift[:, None, :]

def _post_ln(v, g, b):
    return _layernorm(v) * g + b

def _split_cols(p, sizes):
    idx = np.cumsum(np.array(sizes))[:-1].tolist()
    return jnp.split(p, idx, axis=-1)

def _dwconv_centred(u, w, b):
    k = w.shape[0]
    pad = k // 2
    out = lax.conv_general_dilated(u, w[:, None, :], window_strides=(1,), padding=[(pad, pad)],
                                   dimension_numbers=('NWC', 'WIO', 'NWC'),
                                   feature_group_count=u.shape[-1])
    return out + b

def _segsum(a):
    t = a.shape[-1]
    cs = jnp.cumsum(a, axis=-1)
    seg = cs[..., :, None] - cs[..., None, :]
    mask = jnp.tril(jnp.ones((t, t), dtype=bool))
    return jnp.where(mask, seg, -jnp.inf)

def _ssd_scan(xh, dt_raw, bm, cm, a_log, dt_bias):
    bsz, seq, g, r, p = xh.shape
    n = bm.shape[-1]
    q = SSD_CHUNK
    nc = seq // q
    dt = jax.nn.softplus(dt_raw.astype(jnp.float32) + dt_bias.astype(jnp.float32)).reshape(bsz, seq, g, r)
    a = -jnp.exp(a_log.astype(jnp.float32)).reshape(g, r)
    da = (dt * a).reshape(bsz, nc, q, g, r)
    xc = (xh * dt[..., None].astype(xh.dtype)).reshape(bsz, nc, q, g, r, p)
    bc = bm.reshape(bsz, nc, q, g, n)
    cc = cm.reshape(bsz, nc, q, g, n)
    a_cs = jnp.cumsum(da, axis=2)
    seg_l = jnp.exp(_segsum(jnp.transpose(da, (0, 3, 4, 1, 2)))).astype(xh.dtype)
    cb = jnp.einsum('bclgn,bcsgn->bgcls', cc, bc)
    scores = cb[:, :, None] * seg_l
    y_diag = jnp.einsum('bgrcls,bcsgrp->bclgrp', scores, xc)
    decay_states = jnp.exp(a_cs[:, :, -1:] - a_cs).astype(xh.dtype)
    states = jnp.einsum('bclgn,bclgrp->bcgrpn', bc, xc * decay_states[..., None])
    chunk_decay = jnp.exp(a_cs[:, :, -1]).astype(xh.dtype)

    def step(h, inp):
        s_c, d_c = inp
        return h * d_c[..., None, None] + s_c, h

    h0 = jnp.zeros((bsz, g, r, p, n), xh.dtype)
    _, h_in = lax.scan(step, h0, (jnp.moveaxis(states, 1, 0), jnp.moveaxis(chunk_decay, 1, 0)))
    h_in = jnp.moveaxis(h_in, 0, 1)
    decay_out = jnp.exp(a_cs).astype(xh.dtype)
    y_off = jnp.einsum('bclgn,bcgrpn->bclgrp', cc, h_in) * decay_out[..., None]
    return (y_diag + y_off).reshape(bsz, seq, g, r, p)

def _ssd_branch(z, xbc, dt_f, dt_b, conv_w, conv_b, a_log_f, a_log_b, dt_bias_f, dt_bias_b, d_skip, norm_g):
    bsz, seq, _ = z.shape
    xbc = jax.nn.silu(_dwconv_centred(xbc, conv_w, conv_b))
    xs, bm, cm = jnp.split(xbc, [SSD_D_INNER, SSD_D_INNER + SSD_GROUPS * SSD_STATE], axis=-1)
    xh = xs.reshape(bsz, seq, SSD_GROUPS, SSD_HEADS_PER_GROUP, SSD_HEAD_DIM)
    bm = bm.reshape(bsz, seq, SSD_GROUPS, SSD_STATE)
    cm = cm.reshape(bsz, seq, SSD_GROUPS, SSD_STATE)
    flip = lambda t: jnp.flip(t, axis=1)
    y_fwd = _ssd_scan(xh, dt_f, bm, cm, a_log_f, dt_bias_f)
    y_bwd = flip(_ssd_scan(flip(xh), flip(dt_b), flip(bm), flip(cm), a_log_b, dt_bias_b))
    y = y_fwd + y_bwd + xh * d_skip.reshape(SSD_GROUPS, SSD_HEADS_PER_GROUP, 1)
    yg = (y.reshape(bsz, seq, SSD_D_INNER) * jax.nn.silu(z)).reshape(bsz, seq, SSD_GROUPS, SSD_D_INNER // SSD_GROUPS)
    yf = yg.astype(jnp.float32)
    yn = yf * lax.rsqrt(jnp.mean(jnp.square(yf), axis=-1, keepdims=True) + SSD_NORM_EPS)
    return yn.reshape(bsz, seq, SSD_D_INNER).astype(z.dtype) * norm_g

def _pool_branch(u, pool_w, pool_scale):
    bsz, seq, _ = u.shape
    ug = u.reshape(bsz, seq, POOL_GROUPS, POOL_GROUP_DIM)
    cs = jnp.pad(jnp.cumsum(ug.astype(jnp.float32), axis=1), ((0, 0), (1, 0), (0, 0), (0, 0)))
    t = jnp.arange(seq)
    outs = []
    for gi, w in enumerate(POOL_WINDOWS):
        lo = jnp.clip(t - w // 2, 0, seq)
        hi = jnp.clip(t + w // 2, 0, seq)
        cg = cs[:, :, gi]
        cnt = (hi - lo).astype(jnp.float32)[None, :, None]
        outs.append((cg[:, hi] - cg[:, lo]) / cnt)
    pooled = jnp.stack(outs, axis=2).astype(u.dtype)
    mixed = jnp.einsum('bsgc,gcd->bsgd', pooled - ug, pool_w)
    return mixed.reshape(bsz, seq, POOL_WIDTH) * pool_scale

def _hier_moe(h, wg, bg, we, be, w_gate, w_up, w_down):
    bsz, seq, d = h.shape
    tok = h.reshape(bsz * seq, d)
    g_prob = jax.nn.softmax((tok @ wg + bg).astype(jnp.float32), axis=-1)
    g_w, g_idx = lax.top_k(g_prob, 1)
    e_logits = (tok @ we + be).astype(jnp.float32).reshape(-1, MOE_GROUPS, MOE_EXPERTS_PER_GROUP)
    e_in = jnp.take_along_axis(e_logits, g_idx[:, :, None], axis=1)[:, 0]
    e_w, e_idx = lax.top_k(jax.nn.softmax(e_in, axis=-1), MOE_TOP_K)
    e_w = e_w / jnp.sum(e_w, axis=-1, keepdims=True)
    weights = g_w * e_w
    expert_ids = g_idx * MOE_EXPERTS_PER_GROUP + e_idx
    combine = jnp.sum(jax.nn.one_hot(expert_ids, MOE_EXPERTS, dtype=jnp.float32) * weights[..., None],
                      axis=1).astype(tok.dtype)
    out = jnp.zeros_like(tok)
    for e in range(MOE_EXPERTS):
        he = jax.nn.silu(tok @ w_gate[e]) * (tok @ w_up[e])
        out = out + combine[:, e:e + 1] * (he @ w_down[e])
    return out.reshape(bsz, seq, d)

def _dt_bias_init(k, shape):
    dt = jnp.exp(jax.random.uniform(k, shape, jnp.float32, minval=math.log(1e-3), maxval=math.log(1e-1)))
    return dt + jnp.log(-jnp.expm1(-dt))

def setup_inputs(seed: int = 0) -> dict:
    key = jax.random.key(seed)
    ks = jax.random.split(key, 30)
    L = DEPTH

    def nrm(k, shape, scale):
        return jax.random.normal(k, shape, jnp.float32) * scale

    return {
        'x': nrm(ks[0], (BATCH, SEQ, D_MODEL), 1.0),
        'c': nrm(ks[1], (BATCH, D_MODEL), 1.0),
        'w_ada': nrm(ks[2], (L, D_MODEL, N_ADA * D_MODEL), 0.5 * D_MODEL ** -0.5),
        'b_ada': nrm(ks[3], (L, N_ADA * D_MODEL), 0.01),
        'w_in': nrm(ks[4], (L, D_MODEL, IN_PROJ_DIM), D_MODEL ** -0.5),
        'conv_w': nrm(ks[5], (L, SSD_CONV, SSD_CONV_DIM), SSD_CONV ** -0.5),
        'conv_b': nrm(ks[6], (L, SSD_CONV_DIM), 0.01),
        'a_log_f': jnp.log(jax.random.uniform(ks[7], (L, SSD_HEADS), jnp.float32, minval=1.0, maxval=16.0)),
        'a_log_b': jnp.log(jax.random.uniform(ks[8], (L, SSD_HEADS), jnp.float32, minval=1.0, maxval=16.0)),
        'dt_bias_f': _dt_bias_init(ks[9], (L, SSD_HEADS)),
        'dt_bias_b': _dt_bias_init(ks[10], (L, SSD_HEADS)),
        'd_skip': 1.0 + nrm(ks[11], (L, SSD_HEADS), 0.1),
        'ssd_norm_g': 1.0 + nrm(ks[12], (L, SSD_D_INNER), 0.1),
        'w_ssd_out': nrm(ks[13], (L, SSD_D_INNER, D_MODEL), SSD_D_INNER ** -0.5),
        'pool_w': nrm(ks[14], (L, POOL_GROUPS, POOL_GROUP_DIM, POOL_GROUP_DIM), POOL_GROUP_DIM ** -0.5),
        'pool_scale': 1.0 + nrm(ks[15], (L, POOL_WIDTH), 0.1),
        'w_pool_out': nrm(ks[16], (L, POOL_WIDTH, D_MODEL), POOL_WIDTH ** -0.5),
        'gate_b': nrm(ks[17], (L, N_BRANCHES * D_MODEL), 0.01),
        'w_o': nrm(ks[18], (L, D_MODEL, D_MODEL), DEEPNORM_BETA * D_MODEL ** -0.5),
        'ln1_g': 1.0 + nrm(ks[19], (L, D_MODEL), 0.1),
        'ln1_b': nrm(ks[20], (L, D_MODEL), 0.01),
        'router_wg': nrm(ks[21], (L, D_MODEL, MOE_GROUPS), D_MODEL ** -0.5),
        'router_bg': nrm(ks[22], (L, MOE_GROUPS), 0.01),
        'router_we': nrm(ks[23], (L, D_MODEL, MOE_EXPERTS), D_MODEL ** -0.5),
        'router_be': nrm(ks[24], (L, MOE_EXPERTS), 0.01),
        'exp_w_gate': nrm(ks[25], (L, MOE_EXPERTS, D_MODEL, MOE_HIDDEN), D_MODEL ** -0.5),
        'exp_w_up': nrm(ks[26], (L, MOE_EXPERTS, D_MODEL, MOE_HIDDEN), D_MODEL ** -0.5),
        'exp_w_down': nrm(ks[27], (L, MOE_EXPERTS, MOE_HIDDEN, D_MODEL), DEEPNORM_BETA * MOE_HIDDEN ** -0.5),
        'ln2_g': 1.0 + nrm(ks[28], (L, D_MODEL), 0.1),
        'ln2_b': nrm(ks[29], (L, D_MODEL), 0.01),
    }

def reference(x, c, w_ada, b_ada, w_in, conv_w, conv_b, a_log_f, a_log_b, dt_bias_f, dt_bias_b, d_skip,
              ssd_norm_g, w_ssd_out, pool_w, pool_scale, w_pool_out, gate_b, w_o, ln1_g, ln1_b,
              router_wg, router_bg, router_we, router_be, exp_w_gate, exp_w_up, exp_w_down, ln2_g, ln2_b):
    for l in range(DEPTH):
        mod = jax.nn.silu(c) @ w_ada[l] + b_ada[l]
        sh1, sc1, g1, sh2, sc2, g2 = jnp.split(mod, N_ADA, axis=-1)
        h = _modulate(x, sh1, sc1)
        z, xbc, dt_f, dt_b, u_pool, gate_logits = _split_cols(h @ w_in[l], IN_PROJ_SIZES)
        y_ssd = _ssd_branch(z, xbc, dt_f, dt_b, conv_w[l], conv_b[l], a_log_f[l], a_log_b[l],
                            dt_bias_f[l], dt_bias_b[l], d_skip[l], ssd_norm_g[l]) @ w_ssd_out[l]
        y_pool = _pool_branch(u_pool, pool_w[l], pool_scale[l]) @ w_pool_out[l]
        g_ssd, g_pool = jnp.split(jax.nn.sigmoid(gate_logits + gate_b[l]), N_BRANCHES, axis=-1)
        mix = (g_ssd * y_ssd + g_pool * y_pool) @ w_o[l]
        x = _post_ln(DEEPNORM_ALPHA * x + g1[:, None, :] * mix, ln1_g[l], ln1_b[l])
        h2 = _modulate(x, sh2, sc2)
        y_moe = _hier_moe(h2, router_wg[l], router_bg[l], router_we[l], router_be[l],
                          exp_w_gate[l], exp_w_up[l], exp_w_down[l])
        x = _post_ln(DEEPNORM_ALPHA * x + g2[:, None, :] * y_moe, ln2_g[l], ln2_b[l])
    return x


_drawn_inputs = setup_inputs


def setup_inputs(seed=0):
    import zlib

    import numpy as np

    out = dict(_drawn_inputs(seed))
    spreads = {}
    factors = {'b_ada': 8.0,
     'conv_b': 8.0,
     'a_log_f': 24.888,
     'a_log_b': 26.4,
     'dt_bias_f': 22.776,
     'dt_bias_b': 22.784,
     'd_skip': 8.0,
     'ssd_norm_g': 6.294,
     'pool_scale': 6.504,
     'gate_b': 23.997,
     'ln1_b': 5.661,
     'router_bg': 42.211,
     'router_be': 54.935,
     'ln2_b': 5.878}
    for name, (base, spread) in spreads.items():
        noise = np.random.default_rng([zlib.crc32(name.encode()), seed]).standard_normal(out[name].shape)
        drawn = base * np.exp(spread * noise) if base else spread * noise
        out[name] = jnp.asarray(drawn.astype(out[name].dtype))
    for name, factor in factors.items():
        out[name] = (out[name] * factor).astype(out[name].dtype)
    return out
```

```python
from contextlib import ExitStack

import numpy as np

import concourse.bass as bass
from concourse import mybir

F32 = mybir.dt.float32
I32 = mybir.dt.int32
ALU = mybir.AluOpType
ACT = mybir.ActivationFunctionType
AX = mybir.AxisListType

P = 128
T = 256
TT = T // P
D = 1024
KD = D // P
DI = 2 * D
NX = DI // P
GROUPS = 8
HPG = 4
HEADS = GROUPS * HPG
HD = 64
TAPS = 5
PAD = TAPS // 2
CH = 128
NC = T // CH
WINDOWS = (2, 4, 8, 16)
WMAX = max(WINDOWS) // 2
EG, EPG = 4, 8
NE = EG * EPG
HID = 512
KH = HID // P
C = 64
NPAIR = NE // 2
PASSES = T // C
ALPHA = 2.0 ** 0.25
EPS = 1e-5
CW = 512
BIG = 1.0e30

Z0, XBC0 = 0, DI
B0, C0 = XBC0 + DI, XBC0 + DI + GROUPS * P
DT0 = C0 + GROUPS * P
U0 = DT0 + 2 * HEADS
G0 = U0 + D

CONST_COLS = dict(ident=P, tri_f=P, tri_b=P, strict=P, ones=P, every32=P, slot=PASSES * C, rev4=EG, rev8=EPG,
                  edge=len(WINDOWS) * 2 * WMAX)
PARAM_COLS = dict(conv_w=32 * TAPS, conv_b=32, norm_g=NX, pool_scale=KD, gate_b=2 * KD, b_ada=6 * KD, d_skip=NX,
                  c=KD, dt_bias=1, a_log=1)


def columns(widths):
    at, out = 0, {}
    for name, w in widths.items():
        out[name] = (at, at + w)
        at += w
    return out, at


CONST_AT, CONST_W = columns(CONST_COLS)
PARAM_AT, PARAM_W = columns(PARAM_COLS)


def build(nc, t_in, consts_d, params_d, router_b, out_d):
    x_d, w_ada, w_in = t_in["x"][0], t_in["w_ada"][0], t_in["w_in"][0]
    w_gate, w_up, w_down = t_in["exp_w_gate"][0], t_in["exp_w_up"][0], t_in["exp_w_down"][0]
    x_tok_d = x_d.rearrange("(t p) d -> p t d", p=P)
    out_tok_d = out_d[0].rearrange("(t p) d -> p t d", p=P)
    cs_d = nc.dram_tensor("cs_scratch", (2 * HEADS, T), F32, kind="Internal").ap()

    with ExitStack() as ctx:
        arena = ctx.enter_context(nc.sbuf_tensor("arena", [P, 53200], F32))
        banks = [ctx.enter_context(nc.psum_tensor(f"bank{i}", [P, 512], F32)) for i in range(8)]

        def sem(name):
            return ctx.enter_context(nc.semaphore(name))

        KB = 256

        def at(kb, *dims, parts=P):
            start, n = int(kb * KB), int(np.prod(dims))
            view = arena[0:parts, start:start + n]
            if len(dims) == 1:
                return view
            names = "abcd"[:len(dims)]
            return view.rearrange(f"p ({' '.join(names)}) -> p {' '.join(names)}", **dict(zip(names, dims)))

        ring_kb = [0, 16, 32]
        xT = at(48, NX, T)
        BT = at(64, GROUPS, T)
        CT = at(72, GROUPS, T)
        hT = at(80, KD, T)
        decay = [at(kb, 2, HPG, T) for kb in (88, 96, 104)]
        cexp = [at(112 + 4 * i, 2, HPG, CH) for i in range(2)]
        xdt = [at(120 + 4 * i, 2, NC, HPG * HD) for i in range(2)]
        xdec = [at(128 + 2 * i, 2, HPG * HD) for i in range(2)]
        st = [at(132 + 2 * i, 2, HPG * HD) for i in range(2)]
        cbm = at(136, 2, NC, CH)
        xtok = [at(140 + 2 * i, NC, HPG * HD) for i in range(2)]
        btok = [at(144 + i, NC, P) for i in range(2)]
        zT = at(146, NX, T)
        gT = at(162, 2 * KD, T)
        UW = T + 2 * WMAX
        uT = at(178, KD, UW)
        stage_mem = at(112, 3 * 576)
        stage = [at(112 + 2.25 * i, 2, T + 2 * PAD) for i in range(3)]
        w_dt = at(104, KD, 2 * HEADS)
        xtmp = at(146, TT, D)
        xhat = at(154, TT, D)
        row = [at(120 + i, T, parts=2 * HEADS) for i in range(8)]
        CPAD = CH // 2
        scan_mem = at(128, 1024, parts=2 * HEADS)
        scan = [at(128 + 2 * i, NC, CH + 2 * CPAD, parts=2 * HEADS) for i in range(2)]
        rs = at(140, 2, T)
        vtmp = at(142, 2, T)
        psum_buf = [at(195.5 + 1.0625 * i, UW) for i in range(3)]
        consts = at(187, CONST_W)
        params = at(191.5, PARAM_W)
        col = at(193, 5, 2 * HEADS)
        ncol = at(194.25, NC, 2 * HEADS)
        modc = at(194.75, 6 * KD)
        sc1p = at(195, KD)
        sc2p = at(195.03125, KD)
        silu_c = at(195.0625, KD)
        stat = at(195.125, 96)
        c32 = at(195.5, KD, 32)
        ada_sb = at(196.5, CW)
        grow = at(199, 2, D)
        moe_kb = [64, 112, 80, 96, 48, 0, 16, 32]
        ln_g, ln_b = at(128, D), at(132, D)
        tmp_row = at(136, D)
        x1 = at(178, TT, D)
        xh2 = at(146, TT, D)
        h2T = at(154, KD, T)
        ysb = [at(154 + 4 * i, 2, 512) for i in range(2)]
        xe = [at(162 + 4 * i, KD, P) for i in range(2)]
        hs = at(170, HID)
        hm = at(172, HID)
        hTs = at(174, KH, P)
        selT = [at(176, T), at(177, T)]
        w_r = at(140, KD, EG + NE)
        r_bias = at(141.25, EG + NE)
        lg = at(141.5, TT, EG + NE)
        comb = at(142, TT, NE)
        msk = at(142.5, TT, NE)
        rk = at(143, TT, NE)
        passes_i = at(146 - 1 / 256, 1).bitcast(I32)
        r_t = at(143.5, 636)
        sel = [at(186, TT, P), at(193, TT, P)]
        alpha_ident = at(198.5, P)
        selw = [at(196.5, TT, P), at(197.5, TT, P)]

        def const(name):
            a, b = CONST_AT[name]
            return consts[:, a:b]

        def param(name):
            a, b = PARAM_AT[name]
            return params[:, a:b]

        ident, tri_f, tri_b = const("ident"), const("tri_f"), const("tri_b")
        strict, ones, every32, slot_no = const("strict"), const("ones"), const("every32"), const("slot")
        edge = const("edge").rearrange("p (w s e) -> p w s e", w=len(WINDOWS), s=2)
        conv_w = param("conv_w").rearrange("p (m k) -> p m k", k=TAPS)

        PAIR_OF = {"B": 0, "C": 4, "x": 8, "z": 16, "u": 24, "g": 28}
        N_CONV = 16
        POOL_ORDER = (3, 2, 1, 0)
        MIX0, POUT0, SOUT0, WO0, N_PAIRS = 36, 40, 44, 48, 52

        ring_full = [sem(f"ring_full{i}") for i in range(len(ring_kb))]
        moe_full = [sem(f"moe_full{i}") for i in range(8)]
        in_consts, in_params, in_x, in_wdt = sem("in_consts"), sem("in_params"), sem("in_x"), sem("in_wdt")
        in_grow, in_resid, in_wr, in_ln = sem("in_grow"), sem("in_resid"), sem("in_wr"), sem("in_ln")
        in_decay = [sem(f"in_decay{i}") for i in range(3)]
        cs_stored, out_stored = sem("cs_stored"), sem("out_stored")
        silu_c_ready, c32_ready, zeros_done = sem("silu_c_ready"), sem("c32_ready"), sem("zeros_done")
        ada_partial, ada_sb_ready, ada_full, ada_done = (sem("ada_partial"), sem("ada_sb_ready"), sem("ada_full"),
                                                         sem("ada_done"))
        var_ready, rstd_ready, xhat_ready = sem("var_ready"), sem("rstd_ready"), sem("xhat_ready")
        xt_psum, h_act, h_dve, mod1_ready = sem("xt_psum"), sem("h_act"), sem("h_dve"), sem("mod1_ready")
        dt_psum, dt_act, dt_dve = sem("dt_psum"), sem("dt_act"), sem("dt_dve")
        scan_in, scan_done, dec_done, rows_done, cols_psum, cols_done = (
            sem("scan_in"), sem("scan_done"), sem("dec_done"), sem("rows_done"), sem("cols_psum"), sem("cols_done"))
        pair_ready, pair_act, pair_dve = sem("pair_ready"), sem("pair_act"), sem("pair_dve")
        conv_steps, conv_silu = sem("conv_steps"), sem("conv_silu")
        b_copied, steps_ready = sem("b_copied"), sem("steps_ready")
        ssd_a, tok_copied, cb_masked, cexp_ready, exp_ready = (sem("ssd_a"), sem("tok_copied"), sem("cb_masked"),
                                                               sem("cexp_ready"), sem("exp_ready"))
        x_scaled, c_scaled, scores_ready, states_psum, states_sb, y_psum, y_out = (
            sem("x_scaled"), sem("c_scaled"), sem("scores_ready"), sem("states_psum"), sem("states_sb"),
            sem("y_psum"), sem("y_out"))
        pool_sums, pool_diff, gates_ready, z_silu, yg_ready, sq_ready = (
            sem("pool_sums"), sem("pool_diff"), sem("gates_ready"), sem("z_silu"), sem("yg_ready"), sem("sq_ready"))
        gvar_psum, gvar_sb, grstd_ready, grstd_psum, yn_ready, mix_ready = (
            sem("gvar_psum"), sem("gvar_sb"), sem("grstd_ready"), sem("grstd_psum"), sem("yn_ready"),
            sem("mix_ready"))
        xh2_ready, h2_psum, h2_act, h2_dve, lg_psum, ln_gb_used = (
            sem("xh2_ready"), sem("h2_psum"), sem("h2_act"), sem("h2_dve"), sem("lg_psum"), sem("ln_gb_used"))
        rt_dve, rt_act, mask_ready, rank_psum, rank_ready = (
            sem("rt_dve"), sem("rt_act"), sem("mask_ready"), sem("rank_psum"), sem("rank_ready"))
        sel_weighted, sel_ready, gather_half, xe_ready, gate_psum, up_psum, hs_ready, hm_ready = (
            sem("sel_weighted"), sem("sel_ready"), sem("gather_half"), sem("xe_ready"), sem("gate_psum"),
            sem("up_psum"), sem("hs_ready"), sem("hm_ready"))
        selT_psum, selT_sb, hT_psum, hT_sb, yd_psum, y0_sb, y1_sb, scattered = (
            sem("selT_psum"), sem("selT_sb"), sem("hT_psum"), sem("hT_sb"), sem("yd_psum"), sem("y0_sb"),
            sem("y1_sb"), sem("scattered"))
        out_ready, alpha_ident_ready, x1_used = (sem("out_ready"), sem("alpha_ident_ready"), sem("x1_used"))
        passes_ready, more_full, more_free, more_sel, more_gathered, more_xe = (
            sem("passes_ready"), sem("more_full"), sem("more_free"), sem("more_sel"), sem("more_gathered"),
            sem("more_xe"))
        more_gate_up, more_hs, more_hm, more_turned, more_turned_sb, more_down, more_ysb = (
            sem("more_gate_up"), sem("more_hs"), sem("more_hm"), sem("more_turned"), sem("more_turned_sb"),
            sem("more_down"), sem("more_ysb"))
        pool_chain, act_chain, dve_chain = sem("pool_chain"), sem("act_chain"), sem("dve_chain")

        loads = []

        def cols_of(w, c0, n=CW):
            return w[:, c0:c0 + n].rearrange("(k p) n -> p k n", p=P)

        def add_ada(j):
            loads.append(("ada", j, cols_of(w_ada, j * CW), (ada_partial, j + 1)))

        for j in range(4):
            add_ada(j)
        for kind, base, n in (("B", B0, 2), ("C", C0, 2), ("x", XBC0, 4), ("z", Z0, 4), ("u", U0, 2), ("g", G0, 4)):
            for j in range(n):
                loads.append((kind, j, cols_of(w_in, base + j * CW), (pair_ready, PAIR_OF[kind] + 2 * j + 2)))
                if kind in "xz":
                    add_ada(4 + j + (4 if kind == "z" else 0))
        loads.append(("pool_w", 0, t_in["pool_w"][0].rearrange("g (k p) n -> p (g k) n", p=P), (pair_ready, POUT0)))
        for j in range(2):
            loads.append(("pool_out", j, cols_of(t_in["w_pool_out"][0], j * CW), (pair_ready, POUT0 + 2 * j + 2)))
        for j in range(4):
            loads.append(("ssd_out", j, cols_of(t_in["w_ssd_out"][0], j * 256, 256), (pair_ready, SOUT0 + j + 1)))
        for j in range(2):
            loads.append(("w_o", j, cols_of(t_in["w_o"][0], j * CW), (pair_ready, N_PAIRS)))
        NR = len(ring_kb)
        index_of = {(k, i): n for n, (k, i, _, _) in enumerate(loads)}

        def ring_slot(n):
            return at(ring_kb[n % NR], *loads[n][2].shape[1:])

        def loaded(eng, key):
            n = index_of[key]
            eng.wait_ge(ring_full[n % NR], 16 * (n // NR + 1))
            return ring_slot(n)

        def chain(eng, s):
            n = [0]

            def link(ins):
                n[0] += 1
                ins.then_inc(s, 1)
                eng.wait_ge(s, n[0])
            return link

        def moe_src(e, m):
            w = (w_gate, w_up, w_down)[m // 2]
            return w[bass.ds(e + m % 2, 1)].rearrange("o (k p) n -> p (o k) n", p=P)

        def moe_slot(n):
            return at(moe_kb[n % 8], *((KD, CW) if n % 6 < 4 else (KH, D)))

        def moe_loaded(eng, it, q0, m):
            n = 6 * q0 + m
            eng.wait_ge(moe_full[n % 8], 48 * it + 16 * (n // 8 + 1))
            return moe_slot(n)

        def moe_used(eng, it, n):
            q0, kind = n // 6, (n % 6) // 2
            if kind == 0:
                eng.wait_ge(gate_psum, 4 * it + q0 + 1)
            elif kind == 1:
                eng.wait_ge(up_psum, 4 * it + q0 + 1)
            else:
                eng.wait_ge(yd_psum, 8 * it + 2 * q0 + 2)

        def all_pairs(eng, body):
            body(0, 0)
            body(0, 1)
            with eng.Fori(0, 3) as it:
                for u in range(4):
                    body(it, 2 + u)
            body(0, 14)
            body(0, 15)

        def conv_dst(p):
            if p < 4:
                return BT[:, 2 * p:2 * p + 2, :]
            if p < 8:
                return CT[:, 2 * (p - 4):2 * (p - 4) + 2, :]
            return xT[:, 2 * (p - 8):2 * (p - 8) + 2, :]

        def further_passes(eng, step):
            eng.wait_ge(passes_ready, 1)
            passes = eng.value_load(passes_i[0:1, 0:1], min_val=1, max_val=PASSES)
            with eng.If(passes > 1):
                with eng.Fori(1, passes) as b:
                    with eng.Fori(0, NPAIR) as q:
                        step(b, q, NPAIR * (b - 1) + q)

        block = ctx.enter_context(nc.Block())

        @block.sync
        def _(sp):
            def moe_load(it, n):
                e = 8 * it + 2 * (n // 6)
                sp.dma_start(moe_slot(n), moe_src(e, n % 6)).then_inc(moe_full[n % 8], 16)

            sp.dma_start(params, params_d).then_inc(in_params, 16)
            sp.dma_start(consts, consts_d).then_inc(in_consts, 16)
            for n, (kind, i, src, _) in enumerate(loads):
                if n == 1:
                    sp.dma_start(xtmp, x_tok_d).then_inc(in_x, 16)
                if n >= NR:
                    sp.wait_ge(*loads[n - NR][3])
                sp.dma_start(ring_slot(n), src).then_inc(ring_full[n % NR], 16)
                if kind == "pool_out" and i == 1:
                    sp.wait_ge(y_psum, GROUPS)
                    sp.wait_ge(pair_ready, MIX0)
                    for j in range(4):
                        moe_load(0, j)
                if kind == "ssd_out" and i == 0:
                    sp.wait_ge(gvar_psum, 1)
                    moe_load(0, 4)
            sp.wait_ge(pair_ready, N_PAIRS)
            for n in range(5, 8):
                moe_load(0, n)
            with sp.Fori(0, 3) as it:
                for n in range(8, 32):
                    moe_used(sp, it, n - 8)
                    moe_load(it, n)
            for n in range(80, 96):
                moe_used(sp, 0, n - 8)
                moe_load(0, n)

            def reload(b, q, n):
                sp.wait_ge(more_free, n + 1)
                for m in range(6):
                    sp.dma_start(moe_slot(m), moe_src(2 * q, m)).then_inc(more_full, 16)

            further_passes(sp, reload)
            for t in range(TT):
                for n in range(2):
                    cs = slice(n * 512, (n + 1) * 512)
                    sp.wait_ge(out_ready, 2 * t + n + 1)
                    sp.dma_start(out_tok_d[:, t, cs], x1[:, t, cs]).then_inc(out_stored, 16)
            sp.wait_ge(out_stored, 32 * TT)

        @block.gpsimd
        def _(pool):
            link = chain(pool, pool_chain)
            pool.memset(stage_mem, 0.0)
            pool.memset(uT[:, :, :], 0.0)
            pool.memset(scan_mem, 0.0).then_inc(zeros_done, 1)
            pool.wait_ge(zeros_done, 1)
            pool.wait_ge(scan_in, 1)
            cur, sh = 0, 1
            while sh < CH:
                a, b = scan[cur], scan[1 - cur]
                for lo, d in ((0, -sh), (HEADS, sh)):
                    last = pool.tensor_tensor(b[lo:lo + HEADS, :, CPAD:CPAD + CH], a[lo:lo + HEADS, :, CPAD:CPAD + CH],
                                              a[lo:lo + HEADS, :, CPAD + d:CPAD + d + CH], ALU.add)
                link(last)
                cur, sh = 1 - cur, 2 * sh
            pool.tensor_copy(row[6].rearrange("p (c s) -> p c s", c=NC), scan[cur][:, :, CPAD:CPAD + CH])\
                .then_inc(scan_done, 1)
            pool.wait_ge(scan_done, 1)
            pool.dma_start(cs_d, row[6]).then_inc(cs_stored, 16)
            pool.wait_ge(cs_stored, 16)

            def load_decay(g):
                for d in range(2):
                    h0 = d * HEADS + g * HPG
                    pool.dma_start(decay[g % 3][:, d], cs_d[h0:h0 + HPG, :].unsqueeze(0).to_broadcast([P, HPG, T]))\
                        .then_inc(in_decay[g % 3], 16)

            holds = [None] * len(psum_buf)
            n_sums = [0]

            def window_sums(o):
                w = POOL_ORDER[o]
                for i in range(2):
                    if o or i:
                        pool.wait_ge(pool_sums, 2 * o + i)
                    lo, hi = 1, UW
                    for s in range(w + 1):
                        n = n_sums[0] % 3
                        n_sums[0] += 1
                        if holds[n] is not None:
                            pool.wait_ge(pool_diff, holds[n] + 1)
                            holds[n] = None
                        if s == 0:
                            u = uT[:, 2 * w + i, :]
                            left, right = u[:, lo - 1:hi - 1], u[:, lo:hi]
                        else:
                            r = 2 ** (s - 1)
                            lo, hi = lo + r, hi - r
                            half = psum_buf[(n - 1) % 3]
                            left, right = half[:, lo - r:hi - r], half[:, lo + r:hi + r]
                        ins = pool.tensor_tensor(psum_buf[n][:, lo:hi], left, right, ALU.add)
                        if s < w:
                            link(ins)
                        else:
                            ins.then_inc(pool_sums, 1)
                            holds[n] = 2 * o + i

            load_decay(0)
            load_decay(1)
            pool.wait_ge(cols_done, 1)
            load_decay(2)
            for g in range(GROUPS):
                b = g % 2
                pool.wait_ge(tok_copied, g + 1)
                if g >= 2:
                    pool.wait_ge(y_psum, g - 1)
                src = xtok[b].rearrange("p c (h e) -> p c h e", h=HPG)
                for d in range(2):
                    h0 = d * HEADS + g * HPG
                    pool.tensor_tensor(xdt[b][:, d].rearrange("p c (h e) -> p c h e", h=HPG), src,
                                       col[:, 0:NC, h0:h0 + HPG].unsqueeze(3).to_broadcast([P, NC, HPG, HD]), ALU.mult)
                for d in range(2):
                    h0 = d * HEADS + g * HPG
                    last = pool.tensor_tensor(
                        xdec[b][:, d].rearrange("p (h e) -> p h e", h=HPG), src[:, d],
                        col[:, 4, h0:h0 + HPG].unsqueeze(2).to_broadcast([P, HPG, HD]), ALU.mult)
                last.then_inc(x_scaled, 1)
                pool.wait_ge(cexp_ready, g + 1)
                for d in range(2):
                    c = 1 - d
                    last = pool.tensor_tensor(
                        cexp[b][:, d], cexp[b][:, d],
                        CT[:, g, c * CH:(c + 1) * CH].unsqueeze(1).to_broadcast([P, HPG, CH]), ALU.mult)
                last.then_inc(c_scaled, 1)
                if g >= 1 and g + 2 < GROUPS:
                    pool.wait_ge(y_psum, g)
                    load_decay(g + 2)
                if g == 5:
                    pool.wait_ge(pair_act, PAIR_OF["g"])
                    pool.wait_ge(ada_full, 12)
                if g >= 5:
                    window_sums(g - 5)
            window_sums(3)
            def weigh(it, q0):
                b = q0 % 2
                pool.wait_ge(sel_ready, 4 * it + q0 + 1)
                if q0 >= 2:
                    pool.wait_ge(selT_psum, 4 * it + q0 - 1)
                pool.tensor_tensor(selw[b].rearrange("p t (e j) -> p t e j", e=2),
                                   sel[b].rearrange("p t (e j) -> p t e j", e=2),
                                   comb[:, :, bass.ds(8 * it + 2 * q0, 2)].unsqueeze(3).to_broadcast([P, TT, 2, C]),
                                   ALU.mult).then_inc(sel_weighted, 1)

            all_pairs(pool, weigh)

        @block.scalar
        def _(act):
            link = chain(act, act_chain)
            act.wait_ge(in_params, 16)
            act.activation(silu_c, param("c"), ACT.Silu).then_inc(silu_c_ready, 1)
            act.wait_ge(ada_partial, 2)
            act.dma_start(w_dt, w_in[:, DT0:DT0 + 2 * HEADS].rearrange("(k p) n -> p k n", p=P)).then_inc(in_wdt, 16)
            for i in range(2):
                c0 = (2 + 3 * i) * D
                act.dma_start(grow[:, i, :], t_in["b_ada"][:, c0:c0 + D].to_broadcast([P, D])).then_inc(in_grow, 16)

            def sqrt_of(n):
                act.wait_ge(var_ready, n + 1)
                act.activation(stat[:, 24 + n:25 + n], stat[:, 16 + n:17 + n], ACT.Sqrt).then_inc(rstd_ready, 1)

            sqrt_of(0)
            sqrt_of(1)
            act.wait_ge(mod1_ready, 1)
            for j in (0, 2):
                act.wait_ge(xt_psum, j + 1)
                for i in range(2):
                    k = 2 * j + i
                    last = act.activation(hT[:, k, :], banks[j][:, i * T:(i + 1) * T], ACT.Identity,
                                          scale=sc1p[:, k:k + 1], bias=modc[:, k:k + 1])
            last.then_inc(h_act, 1)
            act.wait_ge(dt_psum, 1)
            act.activation(row[0], banks[3][0:2 * HEADS, 0:T], ACT.Identity,
                           bias=params[0:2 * HEADS, PARAM_AT["dt_bias"][0]:PARAM_AT["dt_bias"][1]])
            act.activation(stat[0:2 * HEADS, 60:61], params[0:2 * HEADS, PARAM_AT["a_log"][0]:PARAM_AT["a_log"][1]],
                           ACT.Exp).then_inc(dt_act, 1)
            act.wait_ge(dt_dve, 1)
            act.activation(row[2], row[1], ACT.Exp, scale=-1.0).then_inc(dt_act, 1)
            act.wait_ge(dt_dve, 2)
            act.activation(row[4], row[3], ACT.Ln).then_inc(dt_act, 1)

            def copy_pair(p, dst):
                act.wait_ge(pair_ready, p + 1)
                act.activation(dst, banks[p % 3][:, :].rearrange("p (a t) -> p a t", a=2), ACT.Copy)\
                   .then_inc(pair_act, 1)

            def silu_pair(p):
                act.wait_ge(conv_steps, 2 * TAPS * (p + 1))
                act.activation(conv_dst(p), conv_dst(p), ACT.Silu).then_inc(conv_silu, 1)

            act.wait_ge(zeros_done, 1)
            for p in range(N_CONV):
                if p >= 3:
                    act.wait_ge(conv_steps, 2 * TAPS * (p - 2))
                copy_pair(p, stage[p % 3][:, :, PAD:PAD + T])
                if p == 6:
                    act.wait_ge(scan_done, 1)
                    act.activation(row[5][0:HEADS, 0:CH], row[6][0:HEADS, 0:CH], ACT.Exp, scale=-1.0,
                                   bias=row[6][0:HEADS, CH - 1:CH])
                    act.activation(row[5][HEADS:2 * HEADS, 0:CH], row[6][HEADS:2 * HEADS, CH:T], ACT.Exp, scale=-1.0,
                                   bias=row[6][HEADS:2 * HEADS, CH:CH + 1]).then_inc(dec_done, 1)
                if p >= 1:
                    silu_pair(p - 1)
            silu_pair(N_CONV - 1)
            act.wait_ge(cols_done, 1)

            def group_copies(g):
                b = g % 2
                act.wait_ge(ssd_a, g + 1)
                if g >= 2:
                    act.wait_ge(x_scaled, g - 1)
                    act.wait_ge(states_psum, g - 1)
                act.activation(btok[b], banks[4][:, 256:512].rearrange("p (c n) -> p c n", c=NC),
                               ACT.Copy).then_inc(b_copied, 1)
                act.activation(xtok[b], banks[6][:, :].rearrange("p (c n) -> p c n", c=NC), ACT.Copy)\
                   .then_inc(tok_copied, 1)

            def carried_exps(g):
                act.wait_ge(in_decay[g % 3], 32 * (g // 3 + 1))
                if g >= 2:
                    act.wait_ge(y_psum, g - 1)
                act.activation(cexp[g % 2][:, 0], decay[g % 3][:, 0, :, CH:T], ACT.Exp)
                act.activation(cexp[g % 2][:, 1], decay[g % 3][:, 1, :, 0:CH], ACT.Exp).then_inc(cexp_ready, 1)

            def inner_exps(g):
                act.wait_ge(steps_ready, g + 1)
                e = decay[g % 3][:, :, :, :]
                act.activation(e, e, ACT.Exp).then_inc(exp_ready, 1)

            def group_states(g):
                act.wait_ge(states_psum, g + 1)
                if g >= 2:
                    act.wait_ge(y_psum, g - 1)
                act.activation(st[g % 2], banks[5][:, :].rearrange("p (d n) -> p d n", d=2),
                               ACT.Copy).then_inc(states_sb, 1)

            def silu_z(i):
                act.wait_ge(pair_act, PAIR_OF["z"] + 2 * i + 2)
                act.activation(zT[:, 4 * i:4 * i + 4, :], zT[:, 4 * i:4 * i + 4, :], ACT.Silu).then_inc(z_silu, 1)

            def square_y(i):
                act.wait_ge(yg_ready, i + 1)
                act.activation(xT[:, 4 * i:4 * i + 4, :], zT[:, 4 * i:4 * i + 4, :], ACT.Square).then_inc(sq_ready, 1)

            for j in range(10):
                for p in (16 + 2 * j, 17 + 2 * j):
                    if p < PAIR_OF["u"]:
                        t0 = 2 * (p - PAIR_OF["z"])
                        copy_pair(p, zT[:, t0:t0 + 2, :])
                    elif p < PAIR_OF["g"]:
                        t0 = 2 * (p - PAIR_OF["u"])
                        copy_pair(p, uT[:, t0:t0 + 2, WMAX:WMAX + T])
                    else:
                        t0 = 2 * (p - PAIR_OF["g"])
                        copy_pair(p, gT[:, t0:t0 + 2, :])
                if 1 <= j <= GROUPS:
                    inner_exps(j - 1)
                if j < GROUPS:
                    group_copies(j)
                if 1 <= j <= GROUPS:
                    group_states(j - 1)
                if j < GROUPS:
                    carried_exps(j)
                if 3 <= j <= 6:
                    silu_z(j - 3)
                if 6 <= j <= 8:
                    square_y(j - 6)
            square_y(3)
            act.wait_ge(pair_act, MIX0)
            for k in range(2 * KD):
                a = PARAM_AT["gate_b"][0] + k
                last = act.activation(gT[:, k, :], gT[:, k, :], ACT.Sigmoid, bias=params[:, a:a + 1])
            last.then_inc(gates_ready, 1)
            for o, w in enumerate(POOL_ORDER):
                p = MIX0 + o
                act.wait_ge(pair_ready, p + 1)
                for i in range(2):
                    k = 2 * w + i
                    a = PARAM_AT["pool_scale"][0] + k
                    last = act.activation(uT[:, k, 0:T], banks[p % 3][:, i * T:(i + 1) * T], ACT.Identity,
                                          scale=params[:, a:a + 1])
                last.then_inc(pair_act, 1)
            act.wait_ge(gvar_sb, 1)
            act.activation(rs, vtmp, ACT.Sqrt).then_inc(grstd_ready, 1)
            act.wait_ge(y_out, GROUPS)
            act.dma_start(ln_g, t_in["ln1_g"].to_broadcast([P, D])).then_inc(in_ln, 16)
            act.dma_start(ln_b, t_in["ln1_b"].to_broadcast([P, D])).then_inc(in_ln, 16)
            act.wait_ge(pair_ready, SOUT0)
            act.dma_start(x1, x_tok_d).then_inc(in_resid, 16)
            act.wait_ge(grstd_psum, 1)
            act.dma_start(w_r[:, :, 0:EG], t_in["router_wg"][0].rearrange("(k p) n -> p k n", p=P)).then_inc(in_wr, 16)
            act.dma_start(w_r[:, :, EG:], t_in["router_we"][0].rearrange("(k p) n -> p k n", p=P)).then_inc(in_wr, 16)
            act.dma_start(r_bias, router_b.to_broadcast([P, EG + NE])).then_inc(in_wr, 16)
            for t in range(TT):
                sqrt_of(2 + 2 * t)
                sqrt_of(3 + 2 * t)
                act.wait_ge(h2_psum, 2 * t + 1)
                for k in range(4):
                    last = act.activation(h2T[:, k, t * P:(t + 1) * P], banks[4 + 2 * t][:, k * P:(k + 1) * P],
                                          ACT.Identity, scale=sc2p[:, k:k + 1], bias=modc[:, 3 * KD + k:3 * KD + k + 1])
                last.then_inc(h2_act, 1)
            act.wait_ge(ln_gb_used, 1)
            act.dma_start(ln_g, t_in["ln2_g"].to_broadcast([P, D])).then_inc(in_ln, 16)
            act.dma_start(ln_b, t_in["ln2_b"].to_broadcast([P, D])).then_inc(in_ln, 16)
            act.wait_ge(rt_dve, 1)
            act.activation(r_t[:, 8:16], r_t[:, 0:8], ACT.Exp).then_inc(rt_act, 1)
            act.wait_ge(rt_dve, 2)
            act.activation(r_t[:, 18:20], r_t[:, 16:18], ACT.Exp).then_inc(rt_act, 1)

            def gathered(it, q0):
                for half in range(2):
                    act.wait_ge(gather_half, 8 * it + 2 * q0 + half + 1)
                    for i in range(4):
                        k = 4 * half + i
                        last = act.activation(xe[q0 % 2][:, k, :], banks[4 + half][:, i * P:(i + 1) * P], ACT.Identity,
                                              scale=sc2p[:, k:k + 1], bias=modc[:, 3 * KD + k:3 * KD + k + 1])
                    last.then_inc(xe_ready, 1)

            def pair(it, q0):
                act.wait_ge(gate_psum, 4 * it + q0 + 1)
                if q0:
                    act.wait_ge(hm_ready, 4 * it + q0)
                act.activation(hs, banks[6][:, :], ACT.Silu).then_inc(hs_ready, 1)
                if q0 != NPAIR - 1:
                    gathered(it, q0 + 1)

            gathered(0, 0)
            all_pairs(act, pair)

            def further(b, q, n):
                act.wait_ge(more_gathered, n + 1)
                for k in range(KD):
                    last = act.activation(xe[0][:, k, :], banks[4 + k // 4][:, (k % 4) * P:(k % 4 + 1) * P],
                                          ACT.Identity, scale=sc2p[:, k:k + 1],
                                          bias=modc[:, 3 * KD + k:3 * KD + k + 1])
                last.then_inc(more_xe, 1)
                act.wait_ge(more_gate_up, n + 1)
                act.activation(hs, banks[6][:, :], ACT.Silu).then_inc(more_hs, 1)

            further_passes(act, further)
            for t in range(TT):
                sqrt_of(6 + t)

        @block.tensor
        def _(pe):
            def ada_part(j):
                w = loaded(pe, ("ada", j))
                if j:
                    pe.wait_ge(ada_done, j)
                for k in range(KD):
                    q = k % 4
                    last = pe.matmul(banks[7][32 * q:32 * q + 32, :], c32[:, k, :], w[:, k, :], start=(k < 4),
                                     stop=(k >= 4))
                last.then_inc(ada_partial, 1)

            def ada_whole(j):
                pe.wait_ge(ada_sb_ready, j + 1)
                if j // 2 in (2, 5):
                    last = pe.matmul(banks[7][:, :], every32, ada_sb, start=True, stop=True)
                else:
                    for i in range(4):
                        last = pe.transpose(banks[7][:, i * P:(i + 1) * P], ada_sb[:, i * P:(i + 1) * P], ident)
                last.then_inc(ada_full, 1)

            pe.wait_ge(c32_ready, 1)
            pe.wait_ge(in_consts, 16)
            for j in range(2):
                ada_part(j)
                ada_whole(j)
            pe.wait_ge(xhat_ready, 1)
            for j in range(4):
                for i in range(2):
                    k = 2 * j + i
                    for t in range(TT):
                        last = pe.transpose(banks[j][:, i * T + t * P:i * T + (t + 1) * P],
                                            xhat[:, t, k * P:(k + 1) * P], ident)
                last.then_inc(xt_psum, 1)
            for j in range(2, 4):
                ada_part(j)
                ada_whole(j)

            pe.wait_ge(h_act, 1)
            pe.wait_ge(h_dve, 1)
            pe.wait_ge(in_wdt, 16)
            for k in range(KD):
                last = pe.matmul(banks[3][0:2 * HEADS, 0:T], w_dt[:, k, :], hT[:, k, :], start=(k == 0),
                                 stop=(k == KD - 1))
            last.then_inc(dt_psum, 1)

            def bank_of(p):
                if p >= 3:
                    if p - 3 < POUT0:
                        pe.wait_ge(pair_act, p - 2)
                    else:
                        pe.wait_ge(pair_dve, p - 2 - POUT0)
                return banks[p % 3]

            def project(p, w, k_tiles, src, first_col=0):
                bank = bank_of(p)
                for i in range(2):
                    c0 = first_col + i * P
                    for k in range(k_tiles):
                        last = pe.matmul(bank[:, i * T:(i + 1) * T], w[:, k, c0:c0 + P], src(k), start=(k == 0),
                                         stop=(k == k_tiles - 1))
                last.then_inc(pair_ready, 1)

            def h_of(k):
                return hT[:, k, :]

            def group_a(g):
                pe.wait_ge(conv_silu, PAIR_OF["x"] + g + 1)
                if g:
                    pe.wait_ge(tok_copied, g)
                    pe.wait_ge(cb_masked, g)
                for c in range(NC):
                    ch = slice(c * CH, (c + 1) * CH)
                    pe.matmul(banks[4][:, ch], BT[:, g, ch], CT[:, g, ch], start=True, stop=True)
                for c in range(NC):
                    ch = slice(c * CH, (c + 1) * CH)
                    pe.transpose(banks[4][:, 256 + c * P:256 + (c + 1) * P], BT[:, g, ch], ident)
                    for i in range(2):
                        last = pe.transpose(banks[6][:, c * 256 + i * P:c * 256 + (i + 1) * P], xT[:, 2 * g + i, ch],
                                            ident)
                last.then_inc(ssd_a, 1)

            def group_b(g):
                b = g % 2
                pe.wait_ge(x_scaled, g + 1)
                pe.wait_ge(cols_done, 1)
                if g:
                    pe.wait_ge(states_sb, g)
                for d in range(2):
                    last = pe.matmul(banks[5][:, d * 256:(d + 1) * 256], btok[b][:, d], xdec[b][:, d], start=True,
                                     stop=True)
                last.then_inc(states_psum, 1)

            def group_c(g):
                b = g % 2
                pe.wait_ge(scores_ready, g + 1)
                pe.wait_ge(c_scaled, g + 1)
                pe.wait_ge(states_sb, g + 1)
                if g:
                    pe.wait_ge(y_out, g)
                for i in range(2):
                    for c in range(NC):
                        o = slice(i * T + c * CH, i * T + (c + 1) * CH)
                        for term in range(3):
                            for half in range(2):
                                r = 2 * i + half
                                hd = slice(r * HD, (r + 1) * HD)
                                if term < 2:
                                    lhs = xdt[b][:, term, c, hd]
                                    rhs = decay[g % 3][:, term, r, c * CH:(c + 1) * CH]
                                else:
                                    lhs, rhs = st[b][:, 1 - c, hd], cexp[b][:, 1 - c, r, :]
                                last = pe.matmul(banks[3][half * HD:(half + 1) * HD, o], lhs, rhs, start=(term == 0),
                                                 stop=(term == 2))
                last.then_inc(y_psum, 1)

            pending = None
            for kind, n in (("B", 2), ("C", 2), ("x", 4), ("z", 4), ("u", 2), ("g", 4)):
                for j in range(n):
                    w = loaded(pe, (kind, j))
                    p = PAIR_OF[kind] + 2 * j
                    project(p, w, KD, h_of)
                    if pending is not None:
                        ada_whole(pending)
                        pending = None
                    project(p + 1, w, KD, h_of, 2 * P)
                    if kind in "xz":
                        pending = 4 + j + (4 if kind == "z" else 0)
                        ada_part(pending)
                    if kind == "x" and j == 0:
                        pe.wait_ge(rows_done, 1)
                        pe.wait_ge(scan_done, 1)
                        for i, (r, c) in enumerate(((0, 0), (0, 1), (6, 0), (6, 1), (7, 0))):
                            last = pe.transpose(banks[5][:, i * 64:(i + 1) * 64], row[r][:, c * CH:(c + 1) * CH],
                                                ident[0:64, 0:64])
                        last.then_inc(cols_psum, 1)
                    slot = (p - PAIR_OF["z"]) // 2
                    if 0 <= slot < GROUPS:
                        group_a(slot)
                    if 1 <= slot <= GROUPS:
                        group_b(slot - 1)
                    if 2 <= slot:
                        group_c(slot - 2)

            w = loaded(pe, ("pool_w", 0))
            for o, g in enumerate(POOL_ORDER):
                pe.wait_ge(pool_diff, 2 * o + 2)
                project(MIX0 + o, w[:, 2 * g:2 * g + 2, :], 2, lambda k: uT[:, 2 * g + k, WMAX:WMAX + T])
            pe.wait_ge(sq_ready, 4)
            for hh in range(2):
                for i in range(2):
                    for q in range(4):
                        last = pe.matmul(banks[4][32 * q:32 * q + 32, hh * T:(hh + 1) * T], ones[:, 0:32],
                                         xT[:, 2 * (4 * hh + q) + i, :], start=(i == 0), stop=(i == 1))
            last.then_inc(gvar_psum, 1)
            pe.wait_ge(pair_act, POUT0)
            for j in range(2):
                w = loaded(pe, ("pool_out", j))
                for i in range(2):
                    if (j, i) == (1, 1):
                        pe.wait_ge(grstd_ready, 1)
                        for hh in range(2):
                            for q in range(4):
                                last = pe.matmul(banks[(5, 6, 7, 3)[q]][:, hh * T:(hh + 1) * T], every32[32 * q:32 * q + 32, :],
                                                 rs[32 * q:32 * q + 32, hh, :], start=True, stop=True)
                        last.then_inc(grstd_psum, 1)
                    project(POUT0 + 2 * j + i, w, KD, lambda k: uT[:, k, 0:T], 2 * i * P)
            pe.wait_ge(yn_ready, 1)
            for j in range(4):
                w = loaded(pe, ("ssd_out", j))
                project(SOUT0 + j, w, NX, lambda k: zT[:, k, :])
            pe.wait_ge(mix_ready, 4)
            for t in range(TT):
                for hf in range(2):
                    w = loaded(pe, ("w_o", hf))
                    bank = bank_of(WO0 + 2 * t + hf)
                    for k in range(KD):
                        last = pe.matmul(bank[:, :], gT[:, k, t * P:(t + 1) * P], w[:, k, :], start=(k == 0),
                                         stop=(k == KD - 1))
                    last.then_inc(pair_ready, 1)
            def router(t):
                pe.wait_ge(xh2_ready, t + 1)
                for half in range(2):
                    for i in range(4):
                        k = 4 * half + i
                        last = pe.transpose(banks[(4, 6)[t] + half][:, i * P:(i + 1) * P],
                                            xh2[:, t, k * P:(k + 1) * P], ident)
                    last.then_inc(h2_psum, 1)
                pe.wait_ge(in_wr, 48)
                pe.wait_ge(h2_act, t + 1)
                pe.wait_ge(h2_dve, t + 1)
                for k in range(KD):
                    last = pe.matmul(banks[4][:, t * 64:t * 64 + EG + NE], h2T[:, k, t * P:(t + 1) * P], w_r[:, k, :],
                                     start=(k == 0), stop=(k == KD - 1))
                last.then_inc(lg_psum, 1)

            def start_sums(t):
                for n in range(2):
                    last = pe.matmul(banks[2 * t + n][:, :], alpha_ident, x1[:, t, n * 512:(n + 1) * 512], start=True,
                                     stop=False, skip_group_check=True)
                last.then_inc(x1_used, 1)

            router(0)
            pe.wait_ge(alpha_ident_ready, 1)
            pe.wait_ge(pair_dve, WO0 + 2 * TT - POUT0)
            start_sums(0)
            router(1)
            start_sums(1)
            pe.wait_ge(mask_ready, 1)
            pe.matmul(banks[5][:, 0:NE], strict, msk[:, 0, :], start=True, stop=True)
            pe.matmul(banks[5][:, NE:2 * NE], ones, msk[:, 0, :], start=True, stop=False)
            pe.matmul(banks[5][:, NE:2 * NE], strict, msk[:, 1, :], start=False, stop=True)
            pe.matmul(banks[5][:, 2 * NE:3 * NE], ones, msk[:, 0, :], start=True, stop=False)
            pe.matmul(banks[5][:, 2 * NE:3 * NE], ones, msk[:, 1, :], start=False, stop=True).then_inc(rank_psum, 1)

            def gather(it, q0):
                pe.wait_ge(sel_ready, 4 * it + q0 + 1)
                for half in range(2):
                    for i in range(4):
                        k = 4 * half + i
                        for t in range(TT):
                            last = pe.matmul(banks[4 + half][:, i * P:(i + 1) * P], xh2[:, t, k * P:(k + 1) * P],
                                             sel[q0 % 2][:, t, :], start=(t == 0), stop=(t == TT - 1))
                    last.then_inc(gather_half, 1)

            gather(0, 0)

            def pair(it, q0):
                q, b = 4 * it + q0, q0 % 2
                pe.wait_ge(xe_ready, 8 * it + 2 * q0 + 2)
                if q0:
                    pe.wait_ge(y0_sb, q)
                for m, bank, done in ((0, banks[6], gate_psum), (2, banks[7], up_psum)):
                    if m == 2 and q0:
                        pe.wait_ge(y1_sb, q)
                    w = [moe_loaded(pe, it, q0, m + e) for e in range(2)]
                    for k in range(KD):
                        for e in range(2):
                            last = pe.matmul(bank[e * C:(e + 1) * C, :], xe[b][:, k, e * C:(e + 1) * C], w[e][:, k, :],
                                             start=(k == 0), stop=(k == KD - 1))
                    last.then_inc(done, 1)
                if q0 != NPAIR - 1:
                    if q0:
                        pe.wait_ge(hT_sb, q)
                        pe.wait_ge(selT_sb, q)
                    gather(it, q0 + 1)
                    pe.wait_ge(xe_ready, 8 * it + 2 * q0 + 4)
                pe.wait_ge(sel_weighted, q + 1)
                for t in range(TT):
                    last = pe.transpose(banks[5][:, t * P:(t + 1) * P], selw[b][:, t, :], ident)
                last.then_inc(selT_psum, 1)
                pe.wait_ge(hm_ready, q + 1)
                for k in range(KH):
                    last = pe.transpose(banks[4][:, k * P:(k + 1) * P], hm[:, k * P:(k + 1) * P], ident)
                last.then_inc(hT_psum, 1)
                pe.wait_ge(hT_sb, q + 1)
                w = [moe_loaded(pe, it, q0, 4 + e) for e in range(2)]
                for n in range(2):
                    for k in range(KH):
                        for e in range(2):
                            last = pe.matmul(banks[6 + n][e * C:(e + 1) * C, :], hTs[:, k, e * C:(e + 1) * C],
                                             w[e][:, k, n * CW:(n + 1) * CW], start=(k == 0), stop=(k == KH - 1))
                    last.then_inc(yd_psum, 1)
                pe.wait_ge(selT_sb, q + 1)
                for n in range(2):
                    pe.wait_ge((y0_sb, y1_sb)[n], q + 1)
                    for t in range(TT):
                        last = pe.matmul(banks[2 * t + n][:, :], selT[b][:, t * P:(t + 1) * P], ysb[b][:, n, :],
                                         start=False, stop=(q0 == NPAIR - 1), skip_group_check=True)
                last.then_inc(scattered, 1)

            all_pairs(pe, pair)

            def further(b, q, n):
                pe.wait_ge(more_sel, 2 * n + 2)
                for k in range(KD):
                    for t in range(TT):
                        last = pe.matmul(banks[4 + k // 4][:, (k % 4) * P:(k % 4 + 1) * P],
                                         xh2[:, t, k * P:(k + 1) * P], sel[0][:, t, :], start=(t == 0),
                                         stop=(t == TT - 1))
                last.then_inc(more_gathered, 1)
                pe.wait_ge(more_full, 96 * (n + 1))
                pe.wait_ge(more_xe, n + 1)
                for m, bank in ((0, banks[6]), (2, banks[7])):
                    for e in range(2):
                        for k in range(KD):
                            last = pe.matmul(bank[e * C:(e + 1) * C, :], xe[0][:, k, e * C:(e + 1) * C],
                                             moe_slot(m + e)[:, k, :], start=(k == 0), stop=(k == KD - 1))
                last.then_inc(more_gate_up, 1)
                pe.wait_ge(more_hm, n + 1)
                for t in range(TT):
                    pe.transpose(banks[5][:, t * P:(t + 1) * P], selw[0][:, t, :], ident)
                for k in range(KH):
                    last = pe.transpose(banks[4][:, k * P:(k + 1) * P], hm[:, k * P:(k + 1) * P], ident)
                last.then_inc(more_turned, 1)
                pe.wait_ge(more_turned_sb, n + 1)
                for half in range(2):
                    for e in range(2):
                        for k in range(KH):
                            last = pe.matmul(banks[6 + half][e * C:(e + 1) * C, :], hTs[:, k, e * C:(e + 1) * C],
                                             moe_slot(4 + e)[:, k, half * CW:(half + 1) * CW], start=(k == 0),
                                             stop=(k == KH - 1))
                last.then_inc(more_down, 1)
                pe.wait_ge(more_ysb, n + 1)
                for half in range(2):
                    for t in range(TT):
                        last = pe.matmul(banks[2 * t + half][:, :], selT[0][:, t * P:(t + 1) * P],
                                         ysb[0][:, half, :], start=False, stop=True, skip_group_check=True)
                last.then_inc(more_free, 1)

            pe.wait_ge(scattered, NPAIR)
            pe.transpose(banks[4][:, 0:P], ident, ident).then_inc(more_free, 1)
            further_passes(pe, further)

        @block.vector
        def _(dve):
            link = chain(dve, dve_chain)

            def norm_stats(halves, n):
                bn = stat[:, 32:44].rearrange("p (a b) -> p a b", a=2)
                for i in range(2):
                    last = dve.bn_stats(bn[:, i, :], halves[i])
                link(last)
                link(dve.bn_aggr(stat[:, 2 * n:2 * n + 2], stat[:, 32:44]))
                link(dve.tensor_scalar(stat[:, 50:51], stat[:, 2 * n + 1:2 * n + 2], EPS, None, ALU.add))
                dve.reciprocal(stat[:, 16 + n:17 + n], stat[:, 50:51]).then_inc(var_ready, 1)

            def normalise(dst, src, n):
                dve.wait_ge(rstd_ready, n + 1)
                return dve.tensor_scalar(dst, src, stat[:, 2 * n:2 * n + 1], stat[:, 24 + n:25 + n], ALU.subtract,
                                         ALU.mult)

            def centre_scale(dst, src, gain, n):
                return dve.scalar_tensor_tensor(out=dst, in0=src, scalar=stat[:, 2 * n:2 * n + 1], in1=gain,
                                                op0=ALU.subtract, op1=ALU.mult)

            def scale_shift(dst, shift, n):
                dve.wait_ge(rstd_ready, n + 1)
                return dve.scalar_tensor_tensor(out=dst, in0=dst, scalar=stat[:, 24 + n:25 + n], in1=shift,
                                                op0=ALU.mult, op1=ALU.add)

            dve.wait_ge(silu_c_ready, 1)
            dve.tensor_copy(c32, silu_c.unsqueeze(2).to_broadcast([P, KD, 32])).then_inc(c32_ready, 1)
            def ada_copy(j):
                dve.wait_ge(ada_partial, j + 1)
                if j:
                    dve.wait_ge(ada_full, j)
                dve.tensor_copy(ada_sb, banks[7][:, :]).then_inc(ada_sb_ready, 1)

            def ada_finish(j):
                dve.wait_ge(ada_full, j + 1)
                if j // 2 in (2, 5):
                    dst = grow[:, j // 6, (j % 2) * CW:(j % 2 + 1) * CW]
                    dve.wait_ge(in_grow, 32)
                    dve.tensor_tensor(dst, banks[7][:, :], dst, ALU.add).then_inc(ada_done, 1)
                    return
                dst = modc[:, 4 * j:4 * j + 4]
                link(dve.tensor_reduce(dst, banks[7][:, :].rearrange("p (m q r) -> p m q r", m=4, r=32)[:, :, :, 0],
                                       AX.X, ALU.add))
                a = PARAM_AT["b_ada"][0] + 4 * j
                dve.tensor_tensor(dst, dst, params[:, a:a + 4], ALU.add).then_inc(ada_done, 1)

            for j in range(4):
                if j == 0:
                    dve.wait_ge(in_x, 16)
                if j < TT:
                    norm_stats([xtmp[:, j, i * 512:(i + 1) * 512] for i in range(2)], j)
                ada_copy(j)
                if j == 1:
                    for t in range(TT):
                        last = normalise(xhat[:, t, :], xtmp[:, t, :], t)
                    last.then_inc(xhat_ready, 1)
                ada_finish(j)
            dve.wait_ge(ada_done, 4)
            dve.tensor_scalar(sc1p, modc[:, KD:2 * KD], 1.0, None, ALU.add).then_inc(mod1_ready, 1)
            dve.wait_ge(mod1_ready, 1)
            for j in (1, 3):
                dve.wait_ge(xt_psum, j + 1)
                for i in range(2):
                    k = 2 * j + i
                    last = dve.tensor_scalar(hT[:, k, :], banks[j][:, i * T:(i + 1) * T], sc1p[:, k:k + 1],
                                             modc[:, k:k + 1], ALU.mult, ALU.add)
            last.then_inc(h_dve, 1)

            dve.wait_ge(dt_act, 1)
            link(dve.tensor_scalar(row[7], row[0], -1.0, None, ALU.mult))
            dve.tensor_tensor(row[1], row[0], row[7], ALU.max).then_inc(dt_dve, 1)
            dve.wait_ge(dt_act, 2)
            dve.tensor_scalar(row[3], row[2], 1.0, None, ALU.add).then_inc(dt_dve, 1)
            dve.wait_ge(dt_act, 3)
            dve.wait_ge(dt_dve, 2)
            link(dve.tensor_scalar(row[5], row[3], -1.0, None, ALU.add))
            link(dve.tensor_scalar(row[7], row[5], 0.0, None, ALU.is_equal))
            dve.tensor_tensor(row[4], row[4], row[7], ALU.add)
            link(dve.tensor_tensor(row[5], row[5], row[7], ALU.add))
            link(dve.reciprocal(row[5], row[5]))
            link(dve.tensor_tensor(row[2], row[2], row[4], ALU.mult))
            link(dve.tensor_tensor(row[2], row[2], row[5], ALU.mult))
            link(dve.scalar_tensor_tensor(out=row[0], in0=row[0], scalar=0.0, in1=row[2], op0=ALU.max, op1=ALU.add))
            dve.wait_ge(zeros_done, 1)
            dve.tensor_scalar(scan[0][:, :, CPAD:CPAD + CH], row[0].rearrange("p (c s) -> p c s", c=NC),
                              stat[0:2 * HEADS, 60:61], -1.0, ALU.mult, ALU.mult).then_inc(scan_in, 1)

            def conv(p):
                dve.wait_ge(pair_act, p + 1)
                m0 = PAIR_TILE(p)
                n0 = 2 * TAPS * p
                for k in range(TAPS):
                    for i in range(2):
                        m = m0 + i
                        src, dst = stage[p % 3][:, i, k:k + T], conv_dst(p)[:, i, :]
                        if k == 0:
                            a = PARAM_AT["conv_b"][0] + m
                            ins = dve.tensor_scalar(dst, src, conv_w[:, m, 0:1], params[:, a:a + 1], ALU.mult, ALU.add)
                        else:
                            dve.wait_ge(conv_steps, n0 + 2 * k + i - 1)
                            ins = dve.scalar_tensor_tensor(out=dst, in0=src, scalar=conv_w[:, m, k:k + 1], in1=dst,
                                                           op0=ALU.mult, op1=ALU.add)
                        ins.then_inc(conv_steps, 1)

            def PAIR_TILE(p):
                return NX + 2 * p if p < PAIR_OF["x"] else 2 * (p - PAIR_OF["x"])

            for p in range(N_CONV):
                j = (p - PAIR_OF["x"]) // 2
                if p % 2 == 0 and j >= 1:
                    ada_finish(3 + j)
                conv(p)
                if p % 2 and j >= 0:
                    ada_copy(4 + j)
                if p == 7:
                    dve.wait_ge(dec_done, 1)
                    dve.wait_ge(scan_in, 1)
                    dve.tensor_tensor(row[7][0:HEADS, 0:CH], row[0][0:HEADS, 0:CH], row[5][0:HEADS, 0:CH], ALU.mult)
                    dve.tensor_tensor(row[7][HEADS:, 0:CH], row[0][HEADS:, CH:T], row[5][HEADS:, 0:CH],
                                      ALU.mult).then_inc(rows_done, 1)
                if p == 9:
                    dve.wait_ge(cols_psum, 1)
                    link(dve.tensor_copy(col, banks[5][:, 0:320].rearrange("p (a h) -> p a h", a=5)))
                    dve.tensor_scalar(ncol, col[:, 2:4, :], -1.0, None, ALU.mult).then_inc(cols_done, 1)

            def group_mask(g):
                dve.wait_ge(ssd_a, g + 1)
                dve.wait_ge(b_copied, g + 1)
                if g:
                    dve.wait_ge(scores_ready, g)
                for d, tri in enumerate((tri_f, tri_b)):
                    last = dve.tensor_tensor(cbm[:, d], banks[4][:, 0:256].rearrange("p (c l) -> p c l", c=NC),
                                             tri.unsqueeze(1).to_broadcast([P, NC, CH]), ALU.mult)
                last.then_inc(cb_masked, 1)

            def group_steps(g):
                dve.wait_ge(cexp_ready, g + 1)
                for d in range(2):
                    for r in range(HPG):
                        h = d * HEADS + g * HPG + r
                        for c in range(NC):
                            e = decay[g % 3][:, d, r, c * CH:(c + 1) * CH]
                            last = dve.tensor_scalar(e, e, ncol[:, c, h:h + 1], 0.0, ALU.add, ALU.min)
                last.then_inc(steps_ready, 1)

            def group_scores(g):
                dve.wait_ge(exp_ready, g + 1)
                dve.wait_ge(cb_masked, g + 1)
                for d in range(2):
                    e = decay[g % 3][:, d]
                    last = dve.tensor_tensor(e, e, cbm[:, d].rearrange("p c l -> p (c l)").unsqueeze(1).to_broadcast(
                        [P, HPG, T]), ALU.mult)
                last.then_inc(scores_ready, 1)

            def group_out(g):
                dve.wait_ge(y_psum, g + 1)
                for i in range(2):
                    k = 2 * g + i
                    a = PARAM_AT["d_skip"][0] + k
                    last = dve.scalar_tensor_tensor(out=xT[:, k, :], in0=xT[:, k, :], scalar=params[:, a:a + 1],
                                                    in1=banks[3][:, i * T:(i + 1) * T], op0=ALU.mult, op1=ALU.add)
                last.then_inc(y_out, 1)

            def pool_mean(o):
                w = POOL_ORDER[o]
                for i in range(2):
                    n = 2 * w + i
                    dve.wait_ge(pool_sums, 2 * o + i + 1)
                    buf = (sum(2 * (v + 1) for v in POOL_ORDER[:o]) + (i + 1) * (w + 1) - 1) % 3
                    s = psum_buf[buf][:, WMAX:WMAX + T]
                    for side, e0 in ((0, 0), (1, T - WMAX)):
                        last = dve.tensor_tensor(s[:, e0:e0 + WMAX], s[:, e0:e0 + WMAX], edge[:, w, side, :], ALU.mult)
                    link(last)
                    u = uT[:, n, WMAX:WMAX + T]
                    dve.scalar_tensor_tensor(out=u, in0=s, scalar=1.0 / WINDOWS[w], in1=u, op0=ALU.mult,
                                             op1=ALU.subtract).then_inc(pool_diff, 1)

            def gate_y(i):
                dve.wait_ge(y_out, 2 * i + 2)
                dve.wait_ge(z_silu, i + 1)
                dve.tensor_tensor(zT[:, 4 * i:4 * i + 4, :], xT[:, 4 * i:4 * i + 4, :], zT[:, 4 * i:4 * i + 4, :],
                                  ALU.mult).then_inc(yg_ready, 1)

            for j in range(10):
                if j >= 7:
                    pool_mean(j - 7)
                if j <= 4:
                    ada_finish(7 + j)
                if j < 4:
                    ada_copy(8 + j)
                if j == 5:
                    dve.wait_ge(ada_done, 12)
                    link(dve.tensor_scalar(sc2p, modc[:, 4 * KD:5 * KD], 1.0, None, ALU.add))
                if 1 <= j <= GROUPS:
                    group_scores(j - 1)
                if j < GROUPS:
                    group_mask(j)
                if j >= 2:
                    group_out(j - 2)
                if j < GROUPS:
                    group_steps(j)
                if 5 <= j <= 7:
                    gate_y(j - 5)

            pool_mean(3)
            gate_y(3)
            dve.wait_ge(gates_ready, 1)

            def gate_pool(j):
                p = POUT0 + j
                dve.wait_ge(pair_ready, p + 1)
                g = gT[:, KD + 2 * j:KD + 2 * j + 2, :]
                dve.tensor_tensor(g, banks[p % 3][:, :].rearrange("p (a t) -> p a t", a=2), g,
                                  ALU.mult).then_inc(pair_dve, 1)

            dve.wait_ge(gvar_psum, 1)
            link(dve.tensor_scalar(vtmp, banks[4][:, :].rearrange("p (a t) -> p a t", a=2), 1.0 / 256, EPS, ALU.mult,
                                   ALU.add))
            dve.reciprocal(vtmp, vtmp).then_inc(gvar_sb, 1)
            for j in range(3):
                gate_pool(j)
            dve.wait_ge(grstd_psum, 1)
            for k in range(NX):
                g = k // 2
                a = PARAM_AT["norm_g"][0] + k
                last = dve.scalar_tensor_tensor(out=zT[:, k, :], in0=zT[:, k, :], scalar=params[:, a:a + 1],
                                                in1=banks[(5, 6, 7, 3)[g % 4]][:, (g // 4) * T:(g // 4 + 1) * T],
                                                op0=ALU.mult, op1=ALU.mult)
            last.then_inc(yn_ready, 1)
            gate_pool(3)
            for j in range(4):
                p = SOUT0 + j
                dve.wait_ge(pair_ready, p + 1)
                g = gT[:, 2 * j:2 * j + 2, :]
                dve.tensor_tensor(g, banks[p % 3][:, :].rearrange("p (a t) -> p a t", a=2), g,
                                  ALU.mult).then_inc(pair_dve, 1)
                dve.wait_ge(pair_dve, p - POUT0 + 1)
                dve.tensor_tensor(g, g, gT[:, KD + 2 * j:KD + 2 * j + 2, :], ALU.add).then_inc(mix_ready, 1)

            dve.tensor_scalar(alpha_ident, ident, ALPHA, None, ALU.mult).then_inc(alpha_ident_ready, 1)
            dve.wait_ge(in_ln, 32)
            dve.wait_ge(in_resid, 16)
            for t in range(TT):
                for hf in range(2):
                    p, cs = WO0 + 2 * t + hf, slice(hf * 512, (hf + 1) * 512)
                    dve.wait_ge(pair_ready, p + 1)
                    dve.tensor_tensor(tmp_row[:, cs], banks[p % 3][:, :], grow[:, 0, cs], ALU.mult)\
                       .then_inc(pair_dve, 1)
                    dve.wait_ge(pair_dve, p - POUT0 + 1)
                    link(dve.scalar_tensor_tensor(out=x1[:, t, cs], in0=x1[:, t, cs], scalar=ALPHA, in1=tmp_row[:, cs],
                                                  op0=ALU.mult, op1=ALU.add))
                norm_stats([x1[:, t, 0:512], x1[:, t, 512:D]], 2 + 2 * t)
                link(centre_scale(x1[:, t, :], x1[:, t, :], ln_g, 2 + 2 * t))
                ins = scale_shift(x1[:, t, :], ln_b, 2 + 2 * t)
                if t == TT - 1:
                    ins.then_inc(ln_gb_used, 1)
                    dve.wait_ge(ln_gb_used, 1)
                else:
                    link(ins)
                norm_stats([x1[:, t, 0:512], x1[:, t, 512:D]], 3 + 2 * t)
                normalise(xh2[:, t, :], x1[:, t, :], 3 + 2 * t).then_inc(xh2_ready, 1)
                dve.wait_ge(h2_psum, 2 * t + 2)
                for k in range(4, 8):
                    last = dve.tensor_scalar(h2T[:, k, t * P:(t + 1) * P],
                                             banks[5 + 2 * t][:, (k - 4) * P:(k - 3) * P], sc2p[:, k:k + 1],
                                             modc[:, 3 * KD + k:3 * KD + k + 1], ALU.mult, ALU.add)
                last.then_inc(h2_dve, 1)

            def small(a, n, *dims):
                v = r_t[:, a:a + TT * n]
                return v.rearrange("p (t n) -> p t n", t=TT) if not dims else \
                    v.rearrange("p (t g e) -> p t g e", t=TT, g=dims[0])

            def over(v, n):
                return v.to_broadcast([P, TT, n])

            dve.wait_ge(in_wr, 48)
            dve.wait_ge(lg_psum, TT)
            for t in range(TT):
                last = dve.tensor_tensor(lg[:, t, :], banks[4][:, t * 64:t * 64 + EG + NE], r_bias, ALU.add)
            link(last)
            g_lg = lg[:, :, 0:EG]
            e_lg = lg[:, :, EG:].rearrange("p t (g e) -> p t g e", g=EG)
            g_max, g_sum, g_w = small(20, 1), small(22, 1), small(24, 1)
            g_d, g_exp = small(0, EG), small(8, EG)
            link(dve.tensor_reduce(g_max, g_lg, AX.X, ALU.max))
            dve.tensor_tensor(g_d, g_lg, over(g_max, EG), ALU.subtract).then_inc(rt_dve, 1)

            def first_max(onehot, values, maximum, tie, tie_max, rev, n):
                link(dve.tensor_tensor(tie, values, over(maximum, n), ALU.is_equal))
                link(dve.tensor_tensor(tie, tie, rev.unsqueeze(1).to_broadcast([P, TT, n]), ALU.mult))
                link(dve.tensor_reduce(tie_max, tie, AX.X, ALU.max))
                link(dve.tensor_tensor(onehot, tie, over(tie_max, n), ALU.is_equal))

            g_hot = small(40, EG)
            first_max(g_hot, g_lg, g_max, small(32, EG), small(26, 1), const("rev4"), EG)
            picked = small(192, NE, EG)
            e_in, e_in2 = small(48, EPG), small(104, EPG)
            link(dve.tensor_tensor(picked, e_lg, g_hot.unsqueeze(3).to_broadcast([P, TT, EG, EPG]), ALU.mult))
            link(dve.tensor_reduce(e_in, picked.rearrange("p t g e -> p t e g"), AX.X, ALU.add))
            m1, m2, hot1, hot2, tie = small(64, 1), small(68, 1), small(88, EPG), small(120, EPG), small(72, EPG)
            link(dve.tensor_reduce(m1, e_in, AX.X, ALU.max))
            first_max(hot1, e_in, m1, tie, small(66, 1), const("rev8"), EPG)
            link(dve.scalar_tensor_tensor(out=e_in2, in0=hot1, scalar=-BIG, in1=e_in, op0=ALU.mult, op1=ALU.add))
            link(dve.tensor_reduce(m2, e_in2, AX.X, ALU.max))
            dve.tensor_tensor(small(16, 1), m2, m1, ALU.subtract).then_inc(rt_dve, 1)
            first_max(hot2, e_in2, m2, tie, small(66, 1), const("rev8"), EPG)
            dve.wait_ge(rt_act, 1)
            link(dve.tensor_reduce(g_sum, g_exp, AX.X, ALU.add))
            link(dve.reciprocal(g_w, g_sum))
            dve.wait_ge(rt_act, 2)
            den, w1, w2 = small(28, 1), small(30, 1), small(70, 1)
            link(dve.tensor_scalar(den, small(18, 1), 1.0, None, ALU.add))
            link(dve.reciprocal(den, den))
            link(dve.tensor_tensor(w1, den, g_w, ALU.mult))
            link(dve.tensor_tensor(w2, w1, small(18, 1), ALU.mult))
            ew, ew2, ehot = small(136, EPG), small(152, EPG), small(168, EPG)
            dve.tensor_tensor(ew, hot1, over(w1, EPG), ALU.mult)
            dve.tensor_tensor(ehot, hot1, hot2, ALU.add)
            link(dve.tensor_tensor(ew2, hot2, over(w2, EPG), ALU.mult))
            link(dve.tensor_tensor(ew, ew, ew2, ALU.add))
            g_hot4 = g_hot.unsqueeze(3).to_broadcast([P, TT, EG, EPG])
            dve.tensor_tensor(comb.rearrange("p t (g e) -> p t g e", g=EG), g_hot4,
                              ew.unsqueeze(2).to_broadcast([P, TT, EG, EPG]), ALU.mult)
            dve.tensor_tensor(msk.rearrange("p t (g e) -> p t g e", g=EG), g_hot4,
                              ehot.unsqueeze(2).to_broadcast([P, TT, EG, EPG]), ALU.mult).then_inc(mask_ready, 1)
            dve.wait_ge(mask_ready, 1)
            unrouted = small(192, NE)
            link(dve.tensor_scalar(unrouted, msk, -1.0, 1000.0, ALU.add, ALU.mult))
            dve.wait_ge(rank_psum, 1)
            most, over1, over2, over3 = (r_t[:, i:i + 1] for i in (400, 401, 402, 403))
            link(dve.tensor_reduce(most, banks[5][:, 2 * NE:3 * NE], AX.X, ALU.max))
            link(dve.tensor_scalar(over1, most, float(C), 1.0, ALU.is_gt, ALU.add))
            link(dve.scalar_tensor_tensor(out=over2, in0=most, scalar=float(2 * C), in1=over1, op0=ALU.is_gt,
                                          op1=ALU.add))
            link(dve.scalar_tensor_tensor(out=over3, in0=most, scalar=float(3 * C), in1=over2, op0=ALU.is_gt,
                                          op1=ALU.add))
            dve.tensor_copy(passes_i, over3).then_inc(passes_ready, 1)
            dve.tensor_tensor(rk, banks[5][:, 0:2 * NE].rearrange("p (t e) -> p t e", t=TT), unrouted,
                              ALU.add).then_inc(rank_ready, 1)

            def select(it, q0):
                if q0 >= 2:
                    dve.wait_ge(gather_half, 8 * it + 2 * q0 - 2)
                    dve.wait_ge(sel_weighted, 4 * it + q0 - 1)
                dve.tensor_tensor(sel[q0 % 2].rearrange("p t (e j) -> p t e j", e=2),
                                  slot_no[:, 0:C].unsqueeze(1).unsqueeze(1).to_broadcast([P, TT, 2, C]),
                                  rk[:, :, bass.ds(8 * it + 2 * q0, 2)].unsqueeze(3).to_broadcast([P, TT, 2, C]),
                                  ALU.is_equal).then_inc(sel_ready, 1)

            dve.wait_ge(rank_ready, 1)
            select(0, 0)
            select(0, 1)

            def pair(it, q0):
                q, b = 4 * it + q0, q0 % 2
                dve.wait_ge(up_psum, q + 1)
                dve.wait_ge(hs_ready, q + 1)
                if q0:
                    dve.wait_ge(hT_psum, q)
                dve.tensor_tensor(hm, banks[7][:, :], hs, ALU.mult).then_inc(hm_ready, 1)
                dve.wait_ge(selT_psum, q + 1)
                if q0 >= 2:
                    dve.wait_ge(scattered, q - 1)
                dve.tensor_copy(selT[b], banks[5][:, 0:T]).then_inc(selT_sb, 1)
                dve.wait_ge(hT_psum, q + 1)
                if q0:
                    dve.wait_ge(yd_psum, 2 * q)
                dve.tensor_copy(hTs, banks[4][:, :].rearrange("p (k n) -> p k n", k=KH)).then_inc(hT_sb, 1)
                for n, done in enumerate((y0_sb, y1_sb)):
                    dve.wait_ge(yd_psum, 2 * q + n + 1)
                    dve.tensor_tensor(ysb[b][:, n, :], banks[6 + n][:, :], grow[:, 1, n * 512:(n + 1) * 512],
                                      ALU.mult).then_inc(done, 1)
                if q0 < NPAIR - 2:
                    select(it, q0 + 2)

            all_pairs(dve, pair)
            dve.wait_ge(scattered, NPAIR)

            def further(b, q, n):
                dve.wait_ge(more_free, n + 1)
                dve.tensor_tensor(sel[0].rearrange("p t (e j) -> p t e j", e=2),
                                  slot_no[:, bass.ds(b * C, C)].unsqueeze(1).unsqueeze(1).to_broadcast([P, TT, 2, C]),
                                  rk[:, :, bass.ds(2 * q, 2)].unsqueeze(3).to_broadcast([P, TT, 2, C]),
                                  ALU.is_equal).then_inc(more_sel, 1)
                dve.wait_ge(more_sel, 2 * n + 1)
                dve.tensor_tensor(selw[0].rearrange("p t (e j) -> p t e j", e=2),
                                  sel[0].rearrange("p t (e j) -> p t e j", e=2),
                                  comb[:, :, bass.ds(2 * q, 2)].unsqueeze(3).to_broadcast([P, TT, 2, C]),
                                  ALU.mult).then_inc(more_sel, 1)
                dve.wait_ge(more_hs, n + 1)
                dve.tensor_tensor(hm, banks[7][:, :], hs, ALU.mult).then_inc(more_hm, 1)
                dve.wait_ge(more_turned, n + 1)
                dve.tensor_copy(selT[0], banks[5][:, 0:T])
                dve.tensor_copy(hTs, banks[4][:, :].rearrange("p (k n) -> p k n", k=KH)).then_inc(more_turned_sb, 1)
                dve.wait_ge(more_down, n + 1)
                for half in range(2):
                    last = dve.tensor_tensor(ysb[0][:, half, :], banks[6 + half][:, :],
                                             grow[:, 1, half * 512:(half + 1) * 512], ALU.mult)
                last.then_inc(more_ysb, 1)
                dve.wait_ge(more_free, n + 2)

            further_passes(dve, further)
            dve.wait_ge(in_ln, 64)
            dve.wait_ge(x1_used, TT)
            for t in range(TT):
                norm_stats([banks[2 * t][:, :], banks[2 * t + 1][:, :]], 6 + t)
                for n in range(2):
                    cs = slice(n * 512, (n + 1) * 512)
                    last = centre_scale(x1[:, t, cs], banks[2 * t + n][:, :], ln_g[:, cs], 6 + t)
                link(last)
                for n in range(2):
                    cs = slice(n * 512, (n + 1) * 512)
                    scale_shift(x1[:, t, cs], ln_b[:, cs], 6 + t).then_inc(out_ready, 1)


def shape_constants():
    a = {}
    i = np.arange(P)
    a["ident"] = np.eye(P)
    a["tri_f"] = i[:, None] <= i[None, :]
    a["tri_b"] = i[:, None] >= i[None, :]
    a["strict"] = i[:, None] < i[None, :]
    a["ones"] = np.ones((P, P))
    a["every32"] = np.repeat(i[:, None] % 32 == 0, P, 1)
    a["slot"] = np.repeat(np.arange(PASSES * C)[None], P, 0)
    a["rev4"] = np.repeat(np.arange(EG, 0, -1)[None], P, 0)
    a["rev8"] = np.repeat(np.arange(EPG, 0, -1)[None], P, 0)
    t = np.arange(T)
    edge = np.stack([w / (np.minimum(t + w // 2, T) - np.maximum(t - w // 2, 0)) for w in WINDOWS])
    edge = np.stack([edge[:, :WMAX], edge[:, T - WMAX:]], 1).reshape(1, -1)
    a["edge"] = np.repeat(edge, P, 0)
    return np.concatenate([np.asarray(a[k], np.float32) for k in CONST_COLS], 1)


def packed_parameters(inp):
    def cols(v):
        return v.reshape(-1, P).T

    def rows(f, b):
        out = np.zeros((P, 1), np.float32)
        out[0:HEADS, 0], out[HEADS:2 * HEADS, 0] = f, b
        return out

    a = {
        "conv_w": inp["conv_w"][0].reshape(TAPS, 32, P).transpose(2, 1, 0).reshape(P, -1),
        "conv_b": cols(inp["conv_b"][0]), "norm_g": cols(inp["ssd_norm_g"][0]),
        "pool_scale": cols(inp["pool_scale"][0]), "gate_b": cols(inp["gate_b"][0]), "b_ada": cols(inp["b_ada"][0]),
        "d_skip": cols(np.repeat(inp["d_skip"][0], HD)), "c": cols(inp["c"][0]),
        "dt_bias": rows(inp["dt_bias_f"][0], inp["dt_bias_b"][0]), "a_log": rows(inp["a_log_f"][0], inp["a_log_b"][0]),
    }
    return np.concatenate([a[k] for k in PARAM_COLS], 1)


STREAMED = ["x", "w_ada", "b_ada", "w_in", "pool_w", "w_pool_out", "w_ssd_out", "w_o", "ln1_g", "ln1_b", "router_wg",
            "router_we", "exp_w_gate", "exp_w_up", "exp_w_down", "ln2_g", "ln2_b"]


def kernel(**inputs):
    import concourse.bacc as bacc
    from concourse.bass_utils import run_bass_kernel_spmd

    inp = {k: np.ascontiguousarray(v) for k, v in inputs.items()}
    nc = bacc.Bacc("TRN2", target_bir_lowering=False, num_devices=1)
    arrays = {k: inp[k] for k in STREAMED}
    arrays["consts"] = shape_constants()
    arrays["params"] = packed_parameters(inp)
    arrays["router_b"] = np.concatenate([inp["router_bg"], inp["router_be"]], 1)
    t = {k: nc.dram_tensor(f"in_{k}", a.shape, F32, kind="ExternalInput").ap() for k, a in arrays.items()}
    out = nc.dram_tensor("out", inp["x"].shape, F32, kind="ExternalOutput").ap()
    build(nc, t, t["consts"], t["params"], t["router_b"], out)
    r = run_bass_kernel_spmd(nc, [{f"in_{k}": a for k, a in arrays.items()}], core_ids=[0])
    return r.results[0]["out"]
```

```python
from contextlib import ExitStack

import numpy as np

import concourse.bass as bass
from concourse import mybir

F32 = mybir.dt.float32
I32 = mybir.dt.int32
F32R = mybir.dt.float32r
ALU = mybir.AluOpType
ACT = mybir.ActivationFunctionType
AX = mybir.AxisListType

P = 128
T = 256
TT = T // P
D = 1024
KD = D // P
DI = 2 * D
NX = DI // P
GROUPS = 8
HPG = 4
HEADS = GROUPS * HPG
HD = 64
TAPS = 5
PAD = TAPS // 2
CH = 128
NC = T // CH
WINDOWS = (2, 4, 8, 16)
WMAX = max(WINDOWS) // 2
EG, EPG = 4, 8
NE = EG * EPG
HID = 512
KH = HID // P
C = 64
NPAIR = NE // 2
PASSES = T // C
ALPHA = 2.0 ** 0.25
EPS = 1e-5
CW = 512
BIG = 1.0e30

Z0, XBC0 = 0, DI
B0, C0 = XBC0 + DI, XBC0 + DI + GROUPS * P
DT0 = C0 + GROUPS * P
U0 = DT0 + 2 * HEADS
G0 = U0 + D

CONST_COLS = dict(ident=P, tri_f=P, tri_b=P, strict=P, ones=P, every32=P, slot=PASSES * C, rev4=EG, rev8=EPG,
                  edge=len(WINDOWS) * 2 * WMAX)
PARAM_COLS = dict(conv_w=32 * TAPS, conv_b=32, norm_g=NX, pool_scale=KD, gate_b=2 * KD, b_ada=6 * KD, d_skip=NX,
                  c=KD, dt_bias=1, a_log=1)


def columns(widths):
    at, out = 0, {}
    for name, w in widths.items():
        out[name] = (at, at + w)
        at += w
    return out, at


CONST_AT, CONST_W = columns(CONST_COLS)
PARAM_AT, PARAM_W = columns(PARAM_COLS)


def build(nc, t_in, consts_d, params_d, router_b, out_d):
    x_d, w_ada, w_in = t_in["x"][0], t_in["w_ada"][0], t_in["w_in"][0]
    w_gate, w_up, w_down = t_in["exp_w_gate"][0], t_in["exp_w_up"][0], t_in["exp_w_down"][0]
    x_tok_d = x_d.rearrange("(t p) d -> p t d", p=P)
    out_tok_d = out_d[0].rearrange("(t p) d -> p t d", p=P)
    cs_d = nc.dram_tensor("cs_scratch", (2 * HEADS, T), F32, kind="Internal").ap()

    with ExitStack() as ctx:
        arena_start = -(-nc.sbuf_base // 32) * 32
        arena = ctx.enter_context(nc.sbuf_tensor("arena", [P, 53200], F32))
        banks = [ctx.enter_context(nc.psum_tensor(f"bank{i}", [P, 512], F32)) for i in range(8)]

        def sem(name):
            return ctx.enter_context(nc.semaphore(name))

        KB = 256

        def at(kb, *dims, parts=P):
            start, n = int(kb * KB), int(np.prod(dims))
            view = arena[0:parts, start:start + n]
            if len(dims) == 1:
                return view
            names = "abcd"[:len(dims)]
            return view.rearrange(f"p ({' '.join(names)}) -> p {' '.join(names)}", **dict(zip(names, dims)))

        def rounded(name, kb, *dims):
            whole = nc.alloc_sbuf_tensor_at(name, [P, *dims], F32R, offset=arena_start + int(kb * 1024))
            return whole[(slice(None),) * (len(dims) + 1)]

        ring_kb = [0, 8, 16, 162, 170]
        w_hi = [rounded(f"w_hi{i}", 24 + 8 * i, KD, 2 * P) for i in range(2)]
        w_lo = [rounded(f"w_lo{i}", kb, KD, 2 * P) for i, kb in enumerate(ring_kb)]
        h_hi, h_lo = rounded("h_hi", 80, KD, T), rounded("h_lo", 40, KD, T)
        u_hi, u_lo = rounded("u_hi", 40, KD, T), rounded("u_lo", 80, KD, T)
        y_hi = [rounded(f"y_hi{i}", 64 + 4 * i, 4, T) for i in range(4)]
        y_lo = [rounded(f"y_lo{i}", 146 + 4 * i, 4, T) for i in range(4)]
        u_full = at(88, KD, T)
        wo_kb = [112, 96]
        mix_hi, mix_lo = rounded("mix_hi", 40, KD, T), rounded("mix_lo", 162, KD, T)
        wo_hi = [[rounded(f"wo_hi{hf}{r}", kb + 8 * r, KD // 2, CW) for r in range(2)] for hf, kb in enumerate((48, 80))]
        wo_lo = [[rounded(f"wo_lo{hf}{r}", wo_kb[hf] + 8 * r, KD // 2, CW) for r in range(2)] for hf in range(2)]
        xT = at(48, NX, T)
        BT = at(64, GROUPS, T)
        CT = at(72, GROUPS, T)
        decay = [at(kb, 2, HPG, T) for kb in (88, 96, 104)]
        cexp = [at(112 + 4 * i, 2, HPG, CH) for i in range(2)]
        xdt = [at(120 + 4 * i, 2, NC, HPG * HD) for i in range(2)]
        xdec = [at(128 + 2 * i, 2, HPG * HD) for i in range(2)]
        st = [at(132 + 2 * i, 2, HPG * HD) for i in range(2)]
        cbm = at(136, 2, NC, CH)
        xtok = [at(140 + 2 * i, NC, HPG * HD) for i in range(2)]
        btok = [at(144 + i, NC, P) for i in range(2)]
        zT = at(146, NX, T)
        gT = at(162, 2 * KD, T)
        UW = T + 2 * WMAX
        uT = at(178, KD, UW)
        stage_mem = at(112, 3 * 576)
        stage = [at(112 + 2.25 * i, 2, T + 2 * PAD) for i in range(3)]
        w_dt = at(104, KD, 2 * HEADS)
        xtmp = at(146, TT, D)
        h_full = at(132, KD, T)
        xhat = at(154, TT, D)
        row = [at(120 + i, T, parts=2 * HEADS) for i in range(8)]
        CPAD = CH // 2
        scan_mem = at(128, 1024, parts=2 * HEADS)
        scan = [at(128 + 2 * i, NC, CH + 2 * CPAD, parts=2 * HEADS) for i in range(2)]
        rs = at(140, 2, T)
        vtmp = at(142, 2, T)
        psum_buf = [at(195.5 + 1.0625 * i, UW) for i in range(3)]
        consts = at(187, CONST_W)
        params = at(191.5, PARAM_W)
        col = at(193, 5, 2 * HEADS)
        ncol = at(194.25, NC, 2 * HEADS)
        modc = at(194.75, 6 * KD)
        sc1p = at(195, KD)
        sc2p = at(195.03125, KD)
        silu_c = at(195.0625, KD)
        stat = at(195.125, 96)
        c32 = at(195.5, KD, 32)
        ada_sb = at(196.5, CW)
        grow = at(199, 2, D)
        moe_kb = [64, 0, 16, 32, 48, 80, 96, 112]
        ln_g, ln_b = at(128, D), at(132, D)
        tmp_row = at(136, D)
        x1 = at(178, TT, D)
        xh2 = at(146, TT, D)
        h2T = at(154, KD, T)
        ysb = [at(154 + 4 * i, 2, 512) for i in range(2)]
        xe = [at(162 + 4 * i, KD, P) for i in range(2)]
        hs = at(170, HID)
        hm = at(172, HID)
        hTs = at(174, KH, P)
        selT = [at(176, T), at(177, T)]
        w_r = at(140, KD, EG + NE)
        r_bias = at(141.25, EG + NE)
        lg = at(141.5, TT, EG + NE)
        comb = at(142, TT, NE)
        msk = at(142.5, TT, NE)
        rk = at(143, TT, NE)
        passes_i = at(146 - 1 / 256, 1).bitcast(I32)
        r_t = at(143.5, 636)
        sel = [at(186, TT, P), at(193, TT, P)]
        alpha_ident = at(198.5, P)
        selw = [at(196.5, TT, P), at(197.5, TT, P)]

        def const(name):
            a, b = CONST_AT[name]
            return consts[:, a:b]

        def param(name):
            a, b = PARAM_AT[name]
            return params[:, a:b]

        ident, tri_f, tri_b = const("ident"), const("tri_f"), const("tri_b")
        strict, ones, every32, slot_no = const("strict"), const("ones"), const("every32"), const("slot")
        edge = const("edge").rearrange("p (w s e) -> p w s e", w=len(WINDOWS), s=2)
        conv_w = param("conv_w").rearrange("p (m k) -> p m k", k=TAPS)

        PAIR_OF = {"B": 0, "C": 4, "x": 8, "z": 16, "u": 24, "g": 28}
        N_CONV = 16
        POOL_ORDER = (3, 2, 1, 0)
        MP = 36
        MIX0, POUT0, SOUT0, WO0, N_PAIRS = 36, 40, 44, 48, 52

        ring_full = [sem(f"ring_full{i}") for i in range(len(ring_kb))]
        moe_full = [sem(f"moe_full{i}") for i in range(8)]
        in_consts, in_params, in_x, in_wdt = sem("in_consts"), sem("in_params"), sem("in_x"), sem("in_wdt")
        in_grow, in_resid, in_wr, in_ln = sem("in_grow"), sem("in_resid"), sem("in_wr"), sem("in_ln")
        in_decay = [sem(f"in_decay{i}") for i in range(3)]
        cs_stored, out_stored = sem("cs_stored"), sem("out_stored")
        silu_c_ready, c32_ready, zeros_done = sem("silu_c_ready"), sem("c32_ready"), sem("zeros_done")
        ada_partial, ada_sb_ready, ada_full, ada_done = (sem("ada_partial"), sem("ada_sb_ready"), sem("ada_full"),
                                                         sem("ada_done"))
        var_ready, rstd_ready, xhat_ready = sem("var_ready"), sem("rstd_ready"), sem("xhat_ready")
        xt_psum, h_act, h_dve, mod1_ready = sem("xt_psum"), sem("h_act"), sem("h_dve"), sem("mod1_ready")
        dt_psum, dt_act, dt_dve = sem("dt_psum"), sem("dt_act"), sem("dt_dve")
        scan_in, scan_done, dec_done, rows_done, cols_psum, cols_done = (
            sem("scan_in"), sem("scan_done"), sem("dec_done"), sem("rows_done"), sem("cols_psum"), sem("cols_done"))
        pair_ready, pair_act, pair_dve = sem("pair_ready"), sem("pair_act"), sem("pair_dve")
        conv_steps, conv_silu = sem("conv_steps"), sem("conv_silu")
        b_copied, steps_ready = sem("b_copied"), sem("steps_ready")
        ssd_a, tok_copied, cb_masked, cexp_ready, exp_ready = (sem("ssd_a"), sem("tok_copied"), sem("cb_masked"),
                                                               sem("cexp_ready"), sem("exp_ready"))
        x_scaled, c_scaled, scores_ready, states_psum, states_sb, y_psum, y_out = (
            sem("x_scaled"), sem("c_scaled"), sem("scores_ready"), sem("states_psum"), sem("states_sb"),
            sem("y_psum"), sem("y_out"))
        pool_sums, pool_diff, z_silu, yg_ready, sq_ready = (
            sem("pool_sums"), sem("pool_diff"), sem("z_silu"), sem("yg_ready"), sem("sq_ready"))
        gvar_psum, gvar_sb, grstd_ready, grstd_psum, yn_ready, mix_ready = (
            sem("gvar_psum"), sem("gvar_sb"), sem("grstd_ready"), sem("grstd_psum"), sem("yn_ready"),
            sem("mix_ready"))
        xh2_ready, h2_psum, h2_act, h2_dve, lg_psum, ln_gb_used = (
            sem("xh2_ready"), sem("h2_psum"), sem("h2_act"), sem("h2_dve"), sem("lg_psum"), sem("ln_gb_used"))
        rt_dve, rt_act, mask_ready, rank_psum, rank_ready = (
            sem("rt_dve"), sem("rt_act"), sem("mask_ready"), sem("rank_psum"), sem("rank_ready"))
        sel_weighted, sel_ready, gather_half, xe_ready, gate_psum, up_psum, hs_ready, hm_ready = (
            sem("sel_weighted"), sem("sel_ready"), sem("gather_half"), sem("xe_ready"), sem("gate_psum"),
            sem("up_psum"), sem("hs_ready"), sem("hm_ready"))
        selT_psum, selT_sb, hT_psum, hT_sb, yd_psum, y0_sb, y1_sb, scattered = (
            sem("selT_psum"), sem("selT_sb"), sem("hT_psum"), sem("hT_sb"), sem("yd_psum"), sem("y0_sb"),
            sem("y1_sb"), sem("scattered"))
        wo_full, ssd_out_even = [sem(f"wo_full{i}") for i in range(2)], sem("ssd_out_even")
        mix_hi_ready, mix_lo_ready, wo_hi_ready, wo_lo_ready = (
            sem("mix_hi_ready"), sem("mix_lo_ready"), sem("wo_hi_ready"), sem("wo_lo_ready"))
        u_hi_ready, u_lo_ready, y_hi_ready, y_lo_ready = (sem("u_hi_ready"), sem("u_lo_ready"), sem("y_hi_ready"),
                                                          sem("y_lo_ready"))
        conv_first = sem("conv_first")
        split_ready, pool_split_ready, h_split = sem("split_ready"), sem("pool_split_ready"), sem("h_split")
        w_hi_ready, h_hi_ready = sem("w_hi_ready"), sem("h_hi_ready")
        last_up, last_down, extra_full, counts_psum = (sem("last_up"), sem("last_down"), sem("extra_full"),
                                                       sem("counts_psum"))
        out_ready, alpha_ident_ready, x1_used = (sem("out_ready"), sem("alpha_ident_ready"), sem("x1_used"))
        passes_ready, more_full, more_free, more_sel, more_gathered, more_xe = (
            sem("passes_ready"), sem("more_full"), sem("more_free"), sem("more_sel"), sem("more_gathered"),
            sem("more_xe"))
        more_gate_up, more_hs, more_hm, more_turned, more_turned_sb, more_down, more_ysb = (
            sem("more_gate_up"), sem("more_hs"), sem("more_hm"), sem("more_turned"), sem("more_turned_sb"),
            sem("more_down"), sem("more_ysb"))
        pool_chain, act_chain, dve_chain = sem("pool_chain"), sem("act_chain"), sem("dve_chain")

        loads = []

        def cols_of(w, c0, n=2 * P):
            return w[:, c0:c0 + n].rearrange("(k p) n -> p k n", p=P)

        def add_ada(j):
            for i in (2 * j, 2 * j + 1):
                loads.append(("ada", i, cols_of(w_ada, 256 * i), (ada_partial, i + 1)))

        for j in range(4):
            add_ada(j)
        splits = []
        for kind, base, n in (("B", B0, 4), ("C", C0, 4), ("x", XBC0, 8), ("z", Z0, 8), ("u", U0, 4), ("g", G0, 8)):
            for i in range(n):
                splits.append(len(loads))
                loads.append((kind, i, cols_of(w_in, base + 256 * i), (pair_ready, PAIR_OF[kind] + i + 1)))
                if kind in "xz" and i % 2:
                    add_ada(4 + i // 2 + (4 if kind == "z" else 0))
        loads.append(("pool_w", 0, t_in["pool_w"][0].rearrange("g (k p) n -> p (g k) n", p=P), (pair_ready, POUT0)))
        for j in range(4):
            splits.append(len(loads))
            loads.append(("pool_out", j, cols_of(t_in["w_pool_out"][0], 256 * j), (pair_ready, POUT0 + j + 1)))
        for i in range(KD):
            splits.append(len(loads))
            used = (pair_ready, SOUT0 + i // 2 + 1) if i % 2 else (ssd_out_even, i // 2 + 1)
            loads.append(("ssd_out", i, cols_of(t_in["w_ssd_out"][0], P * i, P), used))
        index_of = {(k, i): n for n, (k, i, _, _) in enumerate(loads)}
        first = index_of["g", 1]
        slot_of = [(n - first) % (5 if n < first else 3) for n in range(len(loads))]
        turn = [slot_of[:n + 1].count(slot_of[n]) for n in range(len(loads))]
        before = [max((m for m in range(n) if slot_of[m] == slot_of[n]), default=None) for n in range(len(loads))]

        def ring_slot(n):
            return at(ring_kb[slot_of[n]], KD, 2 * P)

        def wait_loaded(eng, n):
            eng.wait_ge(ring_full[slot_of[n]], 16 * turn[n])

        def loaded(eng, key):
            wait_loaded(eng, index_of[key])
            return ring_slot(index_of[key])

        POOL_SPLITS = (MP + 2, MP + 3)

        def rest_ready(m):
            if m in POOL_SPLITS:
                return pool_split_ready, 1 + POOL_SPLITS.index(m)
            return split_ready, m + 1 - sum(v < m for v in POOL_SPLITS)

        def split_by(eng, m):
            n = splits[m]
            eng.wait_ge(w_hi_ready, m + 1)
            eng.tensor_tensor(w_lo[slot_of[n]], ring_slot(n), w_hi[m % 2].bitcast(F32), ALU.subtract)\
               .then_inc(rest_ready(m)[0], 1)

        def w_o_slot(hf):
            return at(wo_kb[hf], KD, CW)

        def chain(eng, s):
            n = [0]

            def link(ins):
                n[0] += 1
                ins.then_inc(s, 1)
                eng.wait_ge(s, n[0])
            return link

        EXTRA = 8
        extra_parts = (at(128, 6, CW), at(199, 2, CW))

        def moe_src(e, m):
            w = (w_gate, w_up, w_down)[m // 2]
            return w[bass.ds(e + m % 2, 1)].rearrange("o (k p) n -> p (o k) n", p=P)

        def place(n):
            return n if n < EXTRA else n - 1

        def moe_slot(n):
            return at(moe_kb[place(n) % 8], *((KD, CW) if n % 6 < 4 else (KH, D)))

        def moe_loaded(eng, it, q0, m):
            n = 6 * q0 + m
            if n == EXTRA:
                eng.wait_ge(extra_full, 32)
                return [extra_parts[k // 6][:, k % 6, :] for k in range(KD)]
            eng.wait_ge(moe_full[place(n) % 8], 48 * it + 16 * (place(n) // 8 + 1))
            slot = moe_slot(n)
            return [slot[:, k, :] for k in range(slot.shape[1])]

        def moe_used(eng, it, n):
            q0, kind = n // 6, (n % 6) // 2
            if kind == 0:
                eng.wait_ge(gate_psum, 4 * it + q0 + 1)
            elif kind == 1:
                eng.wait_ge(up_psum, 4 * it + q0 + 1)
            else:
                eng.wait_ge(yd_psum, 8 * it + 2 * q0 + 2)

        def all_pairs(eng, body):
            body(0, 0)
            body(0, 1)
            with eng.Fori(0, 3) as it:
                for u in range(4):
                    body(it, 2 + u)
            body(0, 14)
            body(0, 15)

        N_STEPS = 2 * (TAPS - 1)

        def tile_of(p):
            return NX + 2 * p if p < PAIR_OF["x"] else 2 * (p - PAIR_OF["x"])

        def conv_dst(p):
            if p < 4:
                return BT[:, 2 * p:2 * p + 2, :]
            if p < 8:
                return CT[:, 2 * (p - 4):2 * (p - 4) + 2, :]
            return xT[:, 2 * (p - 8):2 * (p - 8) + 2, :]

        def further_passes(eng, step):
            eng.wait_ge(passes_ready, 1)
            passes = eng.value_load(passes_i[0:1, 0:1], min_val=1, max_val=PASSES)
            with eng.If(passes > 1):
                with eng.Fori(1, passes) as b:
                    with eng.Fori(0, NPAIR) as q:
                        step(b, q, NPAIR * (b - 1) + q)

        block = ctx.enter_context(nc.Block())

        @block.sync
        def _(sp):
            def moe_load(it, n):
                e = 8 * it + 2 * (n // 6)
                sp.dma_start(moe_slot(n), moe_src(e, n % 6)).then_inc(moe_full[place(n) % 8], 16)

            sp.dma_start(params, params_d).then_inc(in_params, 16)
            sp.dma_start(consts, consts_d).then_inc(in_consts, 16)
            for n, (kind, i, src, _) in enumerate(loads):
                if n == 2:
                    sp.dma_start(xtmp, x_tok_d).then_inc(in_x, 16)
                if before[n] is not None:
                    sp.wait_ge(*loads[before[n]][3])
                sp.dma_start(at(ring_kb[slot_of[n]], *src.shape[1:]), src).then_inc(ring_full[slot_of[n]], 16)
                if kind == "pool_out" and i == 2:
                    sp.wait_ge(y_psum, GROUPS)
                    for hf in range(2):
                        sp.dma_start(w_o_slot(hf), cols_of(t_in["w_o"][0], hf * CW, CW)).then_inc(wo_full[hf], 16)
            sp.wait_ge(pair_ready, WO0)
            for n in range(3):
                moe_load(0, n)
            sp.wait_ge(pair_ready, N_PAIRS)
            for n in range(3, 8):
                moe_load(0, n)
            sp.wait_ge(xh2_ready, TT)
            for k0, part in ((0, extra_parts[0]), (6, extra_parts[1])):
                k1 = k0 + part.shape[1]
                sp.dma_start(part, moe_src(2 * (EXTRA // 6), EXTRA % 6)[:, k0:k1, :]).then_inc(extra_full, 16)
            for n in range(9, 17):
                moe_used(sp, 0, n - 9)
                moe_load(0, n)
            with sp.Fori(0, 3) as it:
                for n in range(17, 41):
                    moe_used(sp, it, n - 8)
                    moe_load(it, n)
            for n in range(89, 92):
                moe_used(sp, 0, n - 8)
                moe_load(0, n)
            for pair_of, halves, rest in (((92, 93), [(slice(4 * i, 4 * i + 4), slice(0, CW)) for i in range(2)], last_up),
                                          ((94, 95), [(slice(0, KH), slice(CW * i, CW * i + CW)) for i in range(2)],
                                           last_down)):
                for half, (rows, cs) in enumerate(halves):
                    for n in pair_of:
                        if half == 0:
                            moe_used(sp, 0, n - 8)
                        sp.dma_start(moe_slot(n)[:, rows, cs], moe_src(2 * (n // 6), n % 6)[:, rows, cs])\
                          .then_inc(rest if half else moe_full[place(n) % 8], 16)

            def reload(b, q, n):
                sp.wait_ge(more_free, n + 1)
                for m in range(6):
                    sp.dma_start(moe_slot(m), moe_src(2 * q, m)).then_inc(more_full, 16)

            further_passes(sp, reload)
            for t in range(TT):
                for n in range(2):
                    cs = slice(n * 512, (n + 1) * 512)
                    sp.wait_ge(out_ready, 2 * t + n + 1)
                    sp.dma_start(out_tok_d[:, t, cs], x1[:, t, cs]).then_inc(out_stored, 16)
            sp.wait_ge(out_stored, 32 * TT)

        @block.gpsimd
        def _(pool):
            link = chain(pool, pool_chain)
            pool.memset(stage_mem, 0.0)
            pool.memset(uT[:, :, :], 0.0)
            pool.memset(scan_mem, 0.0).then_inc(zeros_done, 1)
            pool.wait_ge(zeros_done, 1)
            pool.wait_ge(scan_in, 1)
            cur, sh = 0, 1
            while sh < CH:
                a, b = scan[cur], scan[1 - cur]
                for lo, d in ((0, -sh), (HEADS, sh)):
                    last = pool.tensor_tensor(b[lo:lo + HEADS, :, CPAD:CPAD + CH], a[lo:lo + HEADS, :, CPAD:CPAD + CH],
                                              a[lo:lo + HEADS, :, CPAD + d:CPAD + d + CH], ALU.add)
                link(last)
                cur, sh = 1 - cur, 2 * sh
            pool.tensor_copy(row[6].rearrange("p (c s) -> p c s", c=NC), scan[cur][:, :, CPAD:CPAD + CH])\
                .then_inc(scan_done, 1)
            pool.wait_ge(scan_done, 1)
            pool.dma_start(cs_d, row[6]).then_inc(cs_stored, 16)
            pool.wait_ge(cs_stored, 16)

            def load_decay(g):
                for d in range(2):
                    h0 = d * HEADS + g * HPG
                    pool.dma_start(decay[g % 3][:, d], cs_d[h0:h0 + HPG, :].unsqueeze(0).to_broadcast([P, HPG, T]))\
                        .then_inc(in_decay[g % 3], 16)

            holds = [None] * len(psum_buf)
            n_sums = [0]

            def window_sums(o):
                w = POOL_ORDER[o]
                for i in range(2):
                    if o or i:
                        pool.wait_ge(pool_sums, 2 * o + i)
                    lo, hi = 1, UW
                    for s in range(w + 1):
                        n = n_sums[0] % 3
                        n_sums[0] += 1
                        if holds[n] is not None:
                            pool.wait_ge(pool_diff, holds[n] + 1)
                            holds[n] = None
                        if s == 0:
                            u = uT[:, 2 * w + i, :]
                            left, right = u[:, lo - 1:hi - 1], u[:, lo:hi]
                        else:
                            r = 2 ** (s - 1)
                            lo, hi = lo + r, hi - r
                            half = psum_buf[(n - 1) % 3]
                            left, right = half[:, lo - r:hi - r], half[:, lo + r:hi + r]
                        ins = pool.tensor_tensor(psum_buf[n][:, lo:hi], left, right, ALU.add)
                        if s < w:
                            link(ins)
                        else:
                            ins.then_inc(pool_sums, 1)
                            holds[n] = 2 * o + i

            load_decay(0)
            load_decay(1)
            pool.wait_ge(cols_done, 1)
            load_decay(2)
            for g in range(GROUPS):
                b = g % 2
                pool.wait_ge(tok_copied, g + 1)
                if g >= 2:
                    pool.wait_ge(y_psum, g - 1)
                src = xtok[b].rearrange("p c (h e) -> p c h e", h=HPG)
                for d in range(2):
                    h0 = d * HEADS + g * HPG
                    pool.tensor_tensor(xdt[b][:, d].rearrange("p c (h e) -> p c h e", h=HPG), src,
                                       col[:, 0:NC, h0:h0 + HPG].unsqueeze(3).to_broadcast([P, NC, HPG, HD]), ALU.mult)
                for d in range(2):
                    h0 = d * HEADS + g * HPG
                    last = pool.tensor_tensor(
                        xdec[b][:, d].rearrange("p (h e) -> p h e", h=HPG), src[:, d],
                        col[:, 4, h0:h0 + HPG].unsqueeze(2).to_broadcast([P, HPG, HD]), ALU.mult)
                last.then_inc(x_scaled, 1)
                pool.wait_ge(cexp_ready, g + 1)
                for d in range(2):
                    c = 1 - d
                    last = pool.tensor_tensor(
                        cexp[b][:, d], cexp[b][:, d],
                        CT[:, g, c * CH:(c + 1) * CH].unsqueeze(1).to_broadcast([P, HPG, CH]), ALU.mult)
                last.then_inc(c_scaled, 1)
                if g >= 1 and g + 2 < GROUPS:
                    pool.wait_ge(y_psum, g)
                    load_decay(g + 2)
                if g == 5:
                    pool.wait_ge(pair_act, PAIR_OF["g"])
                    pool.wait_ge(ada_full, 12)
                if g >= 5:
                    window_sums(g - 5)
            window_sums(3)
            for m in POOL_SPLITS:
                split_by(pool, m)
            def weigh(it, q0):
                b = q0 % 2
                pool.wait_ge(sel_ready, 4 * it + q0 + 1)
                if q0 >= 2:
                    pool.wait_ge(selT_psum, 4 * it + q0 - 1)
                pool.tensor_tensor(selw[b].rearrange("p t (e j) -> p t e j", e=2),
                                   sel[b].rearrange("p t (e j) -> p t e j", e=2),
                                   comb[:, :, bass.ds(8 * it + 2 * q0, 2)].unsqueeze(3).to_broadcast([P, TT, 2, C]),
                                   ALU.mult).then_inc(sel_weighted, 1)

            all_pairs(pool, weigh)

        @block.scalar
        def _(act):
            link = chain(act, act_chain)
            act.wait_ge(in_params, 16)
            act.activation(silu_c, param("c"), ACT.Silu).then_inc(silu_c_ready, 1)
            act.wait_ge(ada_partial, 4)
            act.dma_start(w_dt, w_in[:, DT0:DT0 + 2 * HEADS].rearrange("(k p) n -> p k n", p=P)).then_inc(in_wdt, 16)
            def sqrt_of(n):
                act.wait_ge(var_ready, n + 1)
                act.activation(stat[:, 24 + n:25 + n], stat[:, 16 + n:17 + n], ACT.Sqrt).then_inc(rstd_ready, 1)

            sqrt_of(0)
            sqrt_of(1)
            def leading(m):
                if m < len(splits):
                    n = splits[m]
                    wait_loaded(act, n)
                    if m >= 2:
                        act.wait_ge(*loads[splits[m - 2]][3])
                    act.activation(w_hi[m % 2], ring_slot(n), ACT.Copy).then_inc(w_hi_ready, 1)

            leading(0)
            act.wait_ge(mod1_ready, 1)
            for j in (0, 2):
                act.wait_ge(xt_psum, j + 1)
                for i in range(2):
                    k = 2 * j + i
                    last = act.activation(h_full[:, k, :], banks[j][:, i * T:(i + 1) * T], ACT.Identity,
                                          scale=sc1p[:, k:k + 1], bias=modc[:, k:k + 1])
            last.then_inc(h_act, 1)
            act.wait_ge(h_act, 1)
            act.wait_ge(h_dve, 1)
            act.activation(h_hi, h_full, ACT.Copy).then_inc(h_hi_ready, 1)

            leading(1)
            for i in range(2):
                c0 = (2 + 3 * i) * D
                act.dma_start(grow[:, i, :], t_in["b_ada"][:, c0:c0 + D].to_broadcast([P, D])).then_inc(in_grow, 16)
            act.wait_ge(dt_psum, 1)
            act.activation(row[0], banks[3][0:2 * HEADS, 0:T], ACT.Identity,
                           bias=params[0:2 * HEADS, PARAM_AT["dt_bias"][0]:PARAM_AT["dt_bias"][1]])
            act.activation(stat[0:2 * HEADS, 60:61], params[0:2 * HEADS, PARAM_AT["a_log"][0]:PARAM_AT["a_log"][1]],
                           ACT.Exp).then_inc(dt_act, 1)
            act.wait_ge(dt_dve, 1)
            act.activation(row[2], row[1], ACT.Exp, scale=-1.0).then_inc(dt_act, 1)
            act.wait_ge(dt_dve, 2)
            act.activation(row[4], row[3], ACT.Ln).then_inc(dt_act, 1)

            def copy_pair(p, dst):
                act.wait_ge(pair_ready, p + 1)
                act.activation(dst, banks[p % 3][:, :].rearrange("p (a t) -> p a t", a=2), ACT.Copy)\
                   .then_inc(pair_act, 1)

            def silu_pair(p):
                act.wait_ge(conv_steps, N_STEPS * (p + 1))
                act.activation(conv_dst(p), conv_dst(p), ACT.Silu).then_inc(conv_silu, 1)

            act.wait_ge(zeros_done, 1)
            for p in range(N_CONV):
                if p >= 3:
                    act.wait_ge(conv_steps, N_STEPS * (p - 2))
                copy_pair(p, stage[p % 3][:, :, PAD:PAD + T])
                leading(p + 2)
                act.wait_ge(pair_act, p + 1)
                for i in range(2):
                    m, a = tile_of(p) + i, PARAM_AT["conv_b"][0] + tile_of(p) + i
                    last = act.activation(conv_dst(p)[:, i, :], stage[p % 3][:, i, 0:T], ACT.Identity,
                                          scale=conv_w[:, m, 0:1], bias=params[:, a:a + 1])
                last.then_inc(conv_first, 1)
                if p == 6:
                    act.wait_ge(scan_done, 1)
                    act.activation(row[5][0:HEADS, 0:CH], row[6][0:HEADS, 0:CH], ACT.Exp, scale=-1.0,
                                   bias=row[6][0:HEADS, CH - 1:CH])
                    act.activation(row[5][HEADS:2 * HEADS, 0:CH], row[6][HEADS:2 * HEADS, CH:T], ACT.Exp, scale=-1.0,
                                   bias=row[6][HEADS:2 * HEADS, CH:CH + 1]).then_inc(dec_done, 1)
                if p >= 1:
                    silu_pair(p - 1)
            silu_pair(N_CONV - 1)
            act.wait_ge(cols_done, 1)

            def group_copies(g):
                b = g % 2
                act.wait_ge(ssd_a, g + 1)
                if g >= 2:
                    act.wait_ge(x_scaled, g - 1)
                    act.wait_ge(states_psum, g - 1)
                act.activation(btok[b], banks[4][:, 256:512].rearrange("p (c n) -> p c n", c=NC),
                               ACT.Copy).then_inc(b_copied, 1)
                act.activation(xtok[b], banks[6][:, :].rearrange("p (c n) -> p c n", c=NC), ACT.Copy)\
                   .then_inc(tok_copied, 1)

            def carried_exps(g):
                act.wait_ge(in_decay[g % 3], 32 * (g // 3 + 1))
                if g >= 2:
                    act.wait_ge(y_psum, g - 1)
                act.activation(cexp[g % 2][:, 0], decay[g % 3][:, 0, :, CH:T], ACT.Exp)
                act.activation(cexp[g % 2][:, 1], decay[g % 3][:, 1, :, 0:CH], ACT.Exp).then_inc(cexp_ready, 1)

            def inner_exps(g):
                act.wait_ge(steps_ready, g + 1)
                e = decay[g % 3][:, :, :, :]
                act.activation(e, e, ACT.Exp).then_inc(exp_ready, 1)

            def group_states(g):
                act.wait_ge(states_psum, g + 1)
                if g >= 2:
                    act.wait_ge(y_psum, g - 1)
                act.activation(st[g % 2], banks[5][:, :].rearrange("p (d n) -> p d n", d=2),
                               ACT.Copy).then_inc(states_sb, 1)

            def silu_z(i):
                act.wait_ge(pair_act, PAIR_OF["z"] + 2 * i + 2)
                act.activation(zT[:, 4 * i:4 * i + 4, :], zT[:, 4 * i:4 * i + 4, :], ACT.Silu).then_inc(z_silu, 1)

            def square_y(i):
                act.wait_ge(yg_ready, i + 1)
                act.activation(xT[:, 4 * i:4 * i + 4, :], zT[:, 4 * i:4 * i + 4, :], ACT.Square).then_inc(sq_ready, 1)

            for j in range(10):
                for p in (16 + 2 * j, 17 + 2 * j):
                    if p < PAIR_OF["u"]:
                        t0 = 2 * (p - PAIR_OF["z"])
                        copy_pair(p, zT[:, t0:t0 + 2, :])
                    elif p < PAIR_OF["g"]:
                        t0 = 2 * (p - PAIR_OF["u"])
                        copy_pair(p, uT[:, t0:t0 + 2, WMAX:WMAX + T])
                    else:
                        t0 = 2 * (p - PAIR_OF["g"])
                        act.wait_ge(pair_ready, p + 1)
                        for i in range(2):
                            a = PARAM_AT["gate_b"][0] + t0 + i
                            last = act.activation(gT[:, t0 + i, :], banks[p % 3][:, i * T:(i + 1) * T], ACT.Sigmoid,
                                                  bias=params[:, a:a + 1])
                        last.then_inc(pair_act, 1)
                    leading(p + 2)
                    if p % 2 == 0 and 1 <= j <= GROUPS:
                        inner_exps(j - 1)
                if j < GROUPS:
                    group_copies(j)
                if 1 <= j <= GROUPS:
                    group_states(j - 1)
                if j < GROUPS:
                    carried_exps(j)
                if 3 <= j <= 6:
                    silu_z(j - 3)
                if 6 <= j <= 8:
                    square_y(j - 6)
            for o, w in enumerate(POOL_ORDER):
                p = MIX0 + o
                act.wait_ge(pair_ready, p + 1)
                for i in range(2):
                    k = 2 * w + i
                    a = PARAM_AT["pool_scale"][0] + k
                    last = act.activation(u_full[:, k, :], banks[p % 3][:, i * T:(i + 1) * T], ACT.Identity,
                                          scale=params[:, a:a + 1])
                last.then_inc(pair_act, 1)
                if o == 0:
                    square_y(3)
                act.wait_ge(pair_act, p + 1)
                act.activation(u_hi[:, 2 * w:2 * w + 2, :], u_full[:, 2 * w:2 * w + 2, :], ACT.Copy)\
                   .then_inc(u_hi_ready, 1)
            act.wait_ge(gvar_sb, 1)
            act.activation(rs, vtmp, ACT.Sqrt).then_inc(grstd_ready, 1)
            leading(MP + 2)
            for i in range(4):
                if i == 2:
                    leading(MP + 3)
                act.wait_ge(yn_ready, i + 1)
                act.activation(y_hi[i], zT[:, 4 * i:4 * i + 4, :], ACT.Copy)\
                   .then_inc(y_hi_ready, 1)
            act.wait_ge(y_out, GROUPS)
            act.dma_start(ln_g, t_in["ln1_g"].to_broadcast([P, D])).then_inc(in_ln, 16)
            act.dma_start(ln_b, t_in["ln1_b"].to_broadcast([P, D])).then_inc(in_ln, 16)
            act.wait_ge(pair_ready, POUT0)
            act.dma_start(x1, x_tok_d).then_inc(in_resid, 16)
            act.wait_ge(grstd_psum, 1)
            act.dma_start(w_r[:, :, 0:EG], t_in["router_wg"][0].rearrange("(k p) n -> p k n", p=P)).then_inc(in_wr, 16)
            act.dma_start(w_r[:, :, EG:], t_in["router_we"][0].rearrange("(k p) n -> p k n", p=P)).then_inc(in_wr, 16)
            act.dma_start(r_bias, router_b.to_broadcast([P, EG + NE])).then_inc(in_wr, 16)
            leading(MP + 4)
            leading(MP + 5)
            for j in range(4):
                hf, r = j // 2, j % 2
                if r == 0:
                    act.wait_ge(wo_full[hf], 16)
                act.activation(wo_hi[hf][r], w_o_slot(hf)[:, 4 * r:4 * r + 4, :], ACT.Copy).then_inc(wo_hi_ready, 1)
                if j < 3:
                    leading(MP + 6 + 2 * j)
                    leading(MP + 7 + 2 * j)
                act.wait_ge(mix_ready, j + 1)
                act.activation(mix_hi[:, 2 * j:2 * j + 2, :], gT[:, 2 * j:2 * j + 2, :], ACT.Copy)\
                   .then_inc(mix_hi_ready, 1)
            for t in range(TT):
                sqrt_of(2 + 2 * t)
                sqrt_of(3 + 2 * t)
                for k in range(KD if t == 0 else KD // 2):
                    if k % 4 == 0:
                        act.wait_ge(h2_psum, 2 * t + k // 4 + 1)
                    last = act.activation(h2T[:, k, t * P:(t + 1) * P],
                                          banks[4 + 2 * t + k // 4][:, (k % 4) * P:(k % 4 + 1) * P], ACT.Identity,
                                          scale=sc2p[:, k:k + 1], bias=modc[:, 3 * KD + k:3 * KD + k + 1])
                last.then_inc(h2_act, 1)
            act.wait_ge(rt_dve, 1)
            act.activation(r_t[:, 8:16], r_t[:, 0:8], ACT.Exp).then_inc(rt_act, 1)
            act.wait_ge(rt_dve, 2)
            act.activation(r_t[:, 18:20], r_t[:, 16:18], ACT.Exp).then_inc(rt_act, 1)

            def gathered(it, q0):
                for half in range(2):
                    act.wait_ge(gather_half, 8 * it + 2 * q0 + half + 1)
                    for i in range(4):
                        k = 4 * half + i
                        last = act.activation(xe[q0 % 2][:, k, :], banks[4 + half][:, i * P:(i + 1) * P], ACT.Identity,
                                              scale=sc2p[:, k:k + 1], bias=modc[:, 3 * KD + k:3 * KD + k + 1])
                    last.then_inc(xe_ready, 1)

            def pair(it, q0):
                if q0 == NPAIR - 2:
                    act.wait_ge(up_psum, 2)
                    act.dma_start(ln_g, t_in["ln2_g"].to_broadcast([P, D])).then_inc(in_ln, 16)
                    act.dma_start(ln_b, t_in["ln2_b"].to_broadcast([P, D])).then_inc(in_ln, 16)
                act.wait_ge(gate_psum, 4 * it + q0 + 1)
                if q0:
                    act.wait_ge(hm_ready, 4 * it + q0)
                act.activation(hs, banks[6][:, :], ACT.Silu).then_inc(hs_ready, 1)
                if q0 != NPAIR - 1:
                    gathered(it, q0 + 1)

            gathered(0, 0)
            all_pairs(act, pair)

            def further(b, q, n):
                act.wait_ge(more_gathered, n + 1)
                for k in range(KD):
                    last = act.activation(xe[0][:, k, :], banks[4 + k // 4][:, (k % 4) * P:(k % 4 + 1) * P],
                                          ACT.Identity, scale=sc2p[:, k:k + 1],
                                          bias=modc[:, 3 * KD + k:3 * KD + k + 1])
                last.then_inc(more_xe, 1)
                act.wait_ge(more_gate_up, n + 1)
                act.activation(hs, banks[6][:, :], ACT.Silu).then_inc(more_hs, 1)

            further_passes(act, further)
            for t in range(TT):
                sqrt_of(6 + t)

        @block.tensor
        def _(pe):
            def ada_part(j):
                if j:
                    pe.wait_ge(ada_done, j)
                for half in range(2):
                    w = loaded(pe, ("ada", 2 * j + half))
                    for k in range(KD):
                        q = k % 4
                        last = pe.matmul(banks[7][32 * q:32 * q + 32, half * 256:(half + 1) * 256], c32[:, k, :],
                                         w[:, k, :], start=(k < 4), stop=(k >= 4))
                    last.then_inc(ada_partial, 1)

            def ada_whole(j):
                pe.wait_ge(ada_sb_ready, j + 1)
                if j // 2 in (2, 5):
                    last = pe.matmul(banks[7][:, :], every32, ada_sb, start=True, stop=True)
                else:
                    for i in range(4):
                        last = pe.transpose(banks[7][:, i * P:(i + 1) * P], ada_sb[:, i * P:(i + 1) * P], ident)
                last.then_inc(ada_full, 1)

            pe.wait_ge(c32_ready, 1)
            pe.wait_ge(in_consts, 16)
            for j in range(3):
                ada_part(j)
                ada_whole(j)
            pe.wait_ge(xhat_ready, 1)
            for j in range(4):
                for i in range(2):
                    k = 2 * j + i
                    for t in range(TT):
                        last = pe.transpose(banks[j][:, i * T + t * P:i * T + (t + 1) * P],
                                            xhat[:, t, k * P:(k + 1) * P], ident)
                last.then_inc(xt_psum, 1)
            ada_part(3)
            ada_whole(3)

            pe.wait_ge(h_act, 1)
            pe.wait_ge(h_dve, 1)
            pe.wait_ge(in_wdt, 16)
            for k in range(KD):
                last = pe.matmul(banks[3][0:2 * HEADS, 0:T], w_dt[:, k, :], h_full[:, k, :], start=(k == 0),
                                 stop=(k == KD - 1))
            last.then_inc(dt_psum, 1)

            def bank_of(p):
                if p >= 3:
                    if p - 3 < POUT0:
                        pe.wait_ge(pair_act, p - 2)
                    else:
                        pe.wait_ge(pair_dve, p - 2 - POUT0)
                return banks[p % 3]

            def project(p, w, k_tiles, src):
                bank = bank_of(p)
                for i in range(2):
                    c0 = i * P
                    for k in range(k_tiles):
                        last = pe.matmul(bank[:, i * T:(i + 1) * T], w[:, k, c0:c0 + P], src(k), start=(k == 0),
                                         stop=(k == k_tiles - 1))
                last.then_inc(pair_ready, 1)

            def split_tile(out, m, w_cols, tiles, b_hi, b_lo, arrives=lambda k: None):
                a_hi, a_lo = (v.rearrange("p k (h n) -> p (k h) n", h=len(tiles) // KD) for v in
                              (w_hi[m % 2], w_lo[slot_of[splits[m]]]))
                for k in tiles:
                    arrives(k)
                    for i, (a, b) in enumerate(((a_lo, b_hi(k)), (a_hi, b_lo(k)), (a_hi, b_hi(k)))):
                        last = pe.matmul(out, a[:, k, w_cols], b, start=(k == tiles[0] and i == 0),
                                         stop=(k == tiles[-1] and i == 2))
                return last

            def project_split(p, m, b_hi, b_lo, tiles=tuple(range(KD)), arrives=lambda k: None):
                pe.wait_ge(*rest_ready(m))
                bank = bank_of(p)
                for i in range(2):
                    last = split_tile(bank[:, i * T:(i + 1) * T], m, slice(i * P, (i + 1) * P), tiles,
                                      lambda k: b_hi[:, k, :], lambda k: b_lo[:, k, :], arrives)
                last.then_inc(pair_ready, 1)

            def group_a(g):
                pe.wait_ge(conv_silu, PAIR_OF["x"] + g + 1)
                if g:
                    pe.wait_ge(tok_copied, g)
                    pe.wait_ge(cb_masked, g)
                for c in range(NC):
                    ch = slice(c * CH, (c + 1) * CH)
                    pe.matmul(banks[4][:, ch], BT[:, g, ch], CT[:, g, ch], start=True, stop=True)
                for c in range(NC):
                    ch = slice(c * CH, (c + 1) * CH)
                    pe.transpose(banks[4][:, 256 + c * P:256 + (c + 1) * P], BT[:, g, ch], ident)
                    for i in range(2):
                        last = pe.transpose(banks[6][:, c * 256 + i * P:c * 256 + (i + 1) * P], xT[:, 2 * g + i, ch],
                                            ident)
                last.then_inc(ssd_a, 1)

            def group_b(g):
                b = g % 2
                pe.wait_ge(x_scaled, g + 1)
                pe.wait_ge(cols_done, 1)
                if g:
                    pe.wait_ge(states_sb, g)
                for d in range(2):
                    last = pe.matmul(banks[5][:, d * 256:(d + 1) * 256], btok[b][:, d], xdec[b][:, d], start=True,
                                     stop=True)
                last.then_inc(states_psum, 1)

            def group_c(g):
                b = g % 2
                pe.wait_ge(scores_ready, g + 1)
                pe.wait_ge(c_scaled, g + 1)
                pe.wait_ge(states_sb, g + 1)
                if g:
                    pe.wait_ge(y_out, g)
                for i in range(2):
                    for c in range(NC):
                        o = slice(i * T + c * CH, i * T + (c + 1) * CH)
                        for term in range(3):
                            for half in range(2):
                                r = 2 * i + half
                                hd = slice(r * HD, (r + 1) * HD)
                                if term < 2:
                                    lhs = xdt[b][:, term, c, hd]
                                    rhs = decay[g % 3][:, term, r, c * CH:(c + 1) * CH]
                                else:
                                    lhs, rhs = st[b][:, 1 - c, hd], cexp[b][:, 1 - c, r, :]
                                last = pe.matmul(banks[3][half * HD:(half + 1) * HD, o], lhs, rhs, start=(term == 0),
                                                 stop=(term == 2))
                last.then_inc(y_psum, 1)

            pe.wait_ge(h_split, 1)
            pending = None
            for kind, n in (("B", 2), ("C", 2), ("x", 4), ("z", 4), ("u", 2), ("g", 4)):
                for j in range(n):
                    p = PAIR_OF[kind] + 2 * j
                    project_split(p, p, h_hi, h_lo)
                    if pending is not None:
                        ada_whole(pending)
                        pending = None
                    project_split(p + 1, p + 1, h_hi, h_lo)
                    if kind in "xz":
                        pending = 4 + j + (4 if kind == "z" else 0)
                        ada_part(pending)
                    if kind == "x" and j == 0:
                        pe.wait_ge(rows_done, 1)
                        pe.wait_ge(scan_done, 1)
                        for i, (r, c) in enumerate(((0, 0), (0, 1), (6, 0), (6, 1), (7, 0))):
                            last = pe.transpose(banks[5][:, i * 64:(i + 1) * 64], row[r][:, c * CH:(c + 1) * CH],
                                                ident[0:64, 0:64])
                        last.then_inc(cols_psum, 1)
                    slot = (p - PAIR_OF["z"]) // 2
                    if 0 <= slot < GROUPS:
                        group_a(slot)
                    if 1 <= slot <= GROUPS:
                        group_b(slot - 1)
                    if 2 <= slot:
                        group_c(slot - 2)

            w = loaded(pe, ("pool_w", 0))
            for o, g in enumerate(POOL_ORDER):
                pe.wait_ge(pool_diff, 2 * o + 2)
                project(MIX0 + o, w[:, 2 * g:2 * g + 2, :], 2, lambda k: uT[:, 2 * g + k, WMAX:WMAX + T])
            pe.wait_ge(sq_ready, 4)
            for hh in range(2):
                for i in range(2):
                    for q in range(4):
                        last = pe.matmul(banks[4][32 * q:32 * q + 32, hh * T:(hh + 1) * T], ones[:, 0:32],
                                         xT[:, 2 * (4 * hh + q) + i, :], start=(i == 0), stop=(i == 1))
            last.then_inc(gvar_psum, 1)
            u_tiles = [2 * w + i for w in POOL_ORDER for i in range(2)]
            for j in range(4):
                if j == 1:
                    pe.wait_ge(grstd_ready, 1)
                    for hh in range(2):
                        for q in range(4):
                            last = pe.matmul(banks[(5, 6, 7, 3)[q]][:, hh * T:(hh + 1) * T],
                                             every32[32 * q:32 * q + 32, :], rs[32 * q:32 * q + 32, hh, :],
                                             start=True, stop=True)
                    last.then_inc(grstd_psum, 1)
                project_split(POUT0 + j, MP + j, u_hi, u_lo, u_tiles,
                              lambda k: pe.wait_ge(u_lo_ready, u_tiles.index(k) // 2 + 1))
            pe.wait_ge(y_lo_ready, 4)
            for i in range(KD):
                if i % 2 == 0:
                    bank = bank_of(SOUT0 + i // 2)
                pe.wait_ge(*rest_ready(MP + 4 + i))
                split_tile(bank[:, (i % 2) * T:(i % 2 + 1) * T], MP + 4 + i, slice(0, P), range(NX),
                           lambda k: y_hi[k // 4][:, k % 4, :], lambda k: y_lo[k // 4][:, k % 4, :])\
                    .then_inc((ssd_out_even, pair_ready)[i % 2], 1)
            pe.wait_ge(wo_lo_ready, 4)
            for t in range(TT):
                for hf in range(2):
                    bank, tok = bank_of(WO0 + 2 * t + hf), slice(t * P, (t + 1) * P)
                    for k in range(KD):
                        pe.wait_ge(mix_lo_ready, k // 2 + 1)
                        w_h, w_l = (v[hf][k // 4][:, k % 4, :] for v in (wo_hi, wo_lo))
                        for i, (a, b) in enumerate(((mix_lo, w_h), (mix_hi, w_l), (mix_hi, w_h))):
                            last = pe.matmul(bank[:, :], a[:, k, tok], b, start=(k == 0 and i == 0),
                                             stop=(k == KD - 1 and i == 2))
                    last.then_inc(pair_ready, 1)
            def router(t):
                pe.wait_ge(xh2_ready, t + 1)
                for half in range(2):
                    for i in range(4):
                        k = 4 * half + i
                        last = pe.transpose(banks[(4, 6)[t] + half][:, i * P:(i + 1) * P],
                                            xh2[:, t, k * P:(k + 1) * P], ident)
                    last.then_inc(h2_psum, 1)
                pe.wait_ge(in_wr, 48)
                pe.wait_ge(h2_act, t + 1)
                if t:
                    pe.wait_ge(h2_dve, 1)
                for k in range(KD):
                    last = pe.matmul(banks[4][:, t * 64:t * 64 + EG + NE], h2T[:, k, t * P:(t + 1) * P], w_r[:, k, :],
                                     start=(k == 0), stop=(k == KD - 1))
                last.then_inc(lg_psum, 1)

            def start_sums(t):
                for n in range(2):
                    last = pe.matmul(banks[2 * t + n][:, :], alpha_ident, x1[:, t, n * 512:(n + 1) * 512], start=True,
                                     stop=False, skip_group_check=True)
                last.then_inc(x1_used, 1)

            router(0)
            pe.wait_ge(alpha_ident_ready, 1)
            pe.wait_ge(pair_dve, WO0 + 2 * TT - POUT0)
            start_sums(0)
            router(1)
            start_sums(1)
            pe.wait_ge(mask_ready, 1)
            pe.matmul(banks[5][:, 0:NE], strict, msk[:, 0, :], start=True, stop=True)
            pe.matmul(banks[5][:, NE:2 * NE], ones, msk[:, 0, :], start=True, stop=False)
            pe.matmul(banks[5][:, NE:2 * NE], strict, msk[:, 1, :], start=False, stop=True).then_inc(rank_psum, 1)
            pe.matmul(banks[6][:, 0:NE], ones, msk[:, 0, :], start=True, stop=False)
            pe.matmul(banks[6][:, 0:NE], ones, msk[:, 1, :], start=False, stop=True).then_inc(counts_psum, 1)

            def gather(it, q0, half):
                pe.wait_ge(sel_ready, 4 * it + q0 + 1)
                if q0:
                    pe.wait_ge(xe_ready, 8 * it + 2 * q0 + half - 1)
                for i in range(4):
                    k = 4 * half + i
                    for t in range(TT):
                        last = pe.matmul(banks[4 + half][:, i * P:(i + 1) * P], xh2[:, t, k * P:(k + 1) * P],
                                         sel[q0 % 2][:, t, :], start=(t == 0), stop=(t == TT - 1))
                last.then_inc(gather_half, 1)

            for half in range(2):
                gather(0, 0, half)
            pe.wait_ge(passes_ready, 1)

            def scatter(it, q0, n):
                pe.wait_ge((y0_sb, y1_sb)[n], 4 * it + q0 + 1)
                for t in range(TT):
                    last = pe.matmul(banks[2 * t + n][:, :], selT[q0 % 2][:, t * P:(t + 1) * P],
                                     ysb[q0 % 2][:, n, :], start=False, stop=(q0 == NPAIR - 1), skip_group_check=True)
                if n == 1:
                    last.then_inc(scattered, 1)

            def pair(it, q0):
                q, b = 4 * it + q0, q0 % 2
                pe.wait_ge(xe_ready, 8 * it + 2 * q0 + 2)
                if q0:
                    pe.wait_ge(y0_sb, q)
                for m, bank, done in ((0, banks[6], gate_psum), (2, banks[7], up_psum)):
                    if m == 2 and q0:
                        pe.wait_ge(y1_sb, q)
                    w = [moe_loaded(pe, it, q0, m + e) for e in range(2)]
                    for k in range(KD):
                        if q0 == NPAIR - 1 and m == 2 and k == 4:
                            pe.wait_ge(last_up, 32)
                        for e in range(2):
                            last = pe.matmul(bank[e * C:(e + 1) * C, :], xe[b][:, k, e * C:(e + 1) * C], w[e][k],
                                             start=(k == 0), stop=(k == KD - 1))
                    last.then_inc(done, 1)
                if q0 != NPAIR - 1:
                    gather(it, q0 + 1, 0)
                pe.wait_ge(hm_ready, q + 1)
                for k in range(KH):
                    last = pe.transpose(banks[7][:, k * P:(k + 1) * P], hm[:, k * P:(k + 1) * P], ident)
                last.then_inc(hT_psum, 1)
                pe.wait_ge(sel_weighted, q + 1)
                for t in range(TT):
                    last = pe.transpose(banks[6][:, t * P:(t + 1) * P], selw[b][:, t, :], ident)
                last.then_inc(selT_psum, 1)
                if q0 != NPAIR - 1:
                    gather(it, q0 + 1, 1)
                pe.wait_ge(hT_sb, q + 1)
                pe.wait_ge(selT_sb, q + 1)
                w = [moe_loaded(pe, it, q0, 4 + e) for e in range(2)]
                for n in range(2):
                    if q0 == NPAIR - 1 and n == 1:
                        pe.wait_ge(last_down, 32)
                    for k in range(KH):
                        for e in range(2):
                            last = pe.matmul(banks[6 + n][e * C:(e + 1) * C, :], hTs[:, k, e * C:(e + 1) * C],
                                             w[e][k][:, n * CW:(n + 1) * CW], start=(k == 0), stop=(k == KH - 1))
                    last.then_inc(yd_psum, 1)
                    if q0 == NPAIR - 1 and n == 0:
                        scatter(it, q0, 0)
                for n in range(2) if q0 != NPAIR - 1 else (1,):
                    scatter(it, q0, n)

            all_pairs(pe, pair)

            def further(b, q, n):
                pe.wait_ge(more_sel, 2 * n + 2)
                for k in range(KD):
                    for t in range(TT):
                        last = pe.matmul(banks[4 + k // 4][:, (k % 4) * P:(k % 4 + 1) * P],
                                         xh2[:, t, k * P:(k + 1) * P], sel[0][:, t, :], start=(t == 0),
                                         stop=(t == TT - 1))
                last.then_inc(more_gathered, 1)
                pe.wait_ge(more_full, 96 * (n + 1))
                pe.wait_ge(more_xe, n + 1)
                for m, bank in ((0, banks[6]), (2, banks[7])):
                    for e in range(2):
                        for k in range(KD):
                            last = pe.matmul(bank[e * C:(e + 1) * C, :], xe[0][:, k, e * C:(e + 1) * C],
                                             moe_slot(m + e)[:, k, :], start=(k == 0), stop=(k == KD - 1))
                last.then_inc(more_gate_up, 1)
                pe.wait_ge(more_hm, n + 1)
                for t in range(TT):
                    pe.transpose(banks[5][:, t * P:(t + 1) * P], selw[0][:, t, :], ident)
                for k in range(KH):
                    last = pe.transpose(banks[4][:, k * P:(k + 1) * P], hm[:, k * P:(k + 1) * P], ident)
                last.then_inc(more_turned, 1)
                pe.wait_ge(more_turned_sb, n + 1)
                for half in range(2):
                    for e in range(2):
                        for k in range(KH):
                            last = pe.matmul(banks[6 + half][e * C:(e + 1) * C, :], hTs[:, k, e * C:(e + 1) * C],
                                             moe_slot(4 + e)[:, k, half * CW:(half + 1) * CW], start=(k == 0),
                                             stop=(k == KH - 1))
                last.then_inc(more_down, 1)
                pe.wait_ge(more_ysb, n + 1)
                for half in range(2):
                    for t in range(TT):
                        last = pe.matmul(banks[2 * t + half][:, :], selT[0][:, t * P:(t + 1) * P],
                                         ysb[0][:, half, :], start=False, stop=True, skip_group_check=True)
                last.then_inc(more_free, 1)

            pe.wait_ge(scattered, NPAIR)
            pe.transpose(banks[4][:, 0:P], ident, ident).then_inc(more_free, 1)
            further_passes(pe, further)

        @block.vector
        def _(dve):
            link = chain(dve, dve_chain)

            def norm_stats(halves, n):
                bn = stat[:, 32:44].rearrange("p (a b) -> p a b", a=2)
                for i in range(2):
                    last = dve.bn_stats(bn[:, i, :], halves[i])
                link(last)
                link(dve.bn_aggr(stat[:, 2 * n:2 * n + 2], stat[:, 32:44]))
                link(dve.tensor_scalar(stat[:, 50:51], stat[:, 2 * n + 1:2 * n + 2], EPS, None, ALU.add))
                dve.reciprocal(stat[:, 16 + n:17 + n], stat[:, 50:51]).then_inc(var_ready, 1)

            def normalise(dst, src, n):
                dve.wait_ge(rstd_ready, n + 1)
                return dve.tensor_scalar(dst, src, stat[:, 2 * n:2 * n + 1], stat[:, 24 + n:25 + n], ALU.subtract,
                                         ALU.mult)

            def centre_scale(dst, src, gain, n):
                return dve.scalar_tensor_tensor(out=dst, in0=src, scalar=stat[:, 2 * n:2 * n + 1], in1=gain,
                                                op0=ALU.subtract, op1=ALU.mult)

            def scale_shift(dst, shift, n):
                dve.wait_ge(rstd_ready, n + 1)
                return dve.scalar_tensor_tensor(out=dst, in0=dst, scalar=stat[:, 24 + n:25 + n], in1=shift,
                                                op0=ALU.mult, op1=ALU.add)

            dve.wait_ge(silu_c_ready, 1)
            dve.tensor_copy(c32, silu_c.unsqueeze(2).to_broadcast([P, KD, 32])).then_inc(c32_ready, 1)
            def ada_copy(j):
                dve.wait_ge(ada_partial, 2 * j + 2)
                if j:
                    dve.wait_ge(ada_full, j)
                dve.tensor_copy(ada_sb, banks[7][:, :]).then_inc(ada_sb_ready, 1)

            def ada_finish(j):
                dve.wait_ge(ada_full, j + 1)
                if j // 2 in (2, 5):
                    dst = grow[:, j // 6, (j % 2) * CW:(j % 2 + 1) * CW]
                    dve.wait_ge(in_grow, 32)
                    dve.tensor_tensor(dst, banks[7][:, :], dst, ALU.add).then_inc(ada_done, 1)
                    return
                dst = modc[:, 4 * j:4 * j + 4]
                link(dve.tensor_reduce(dst, banks[7][:, :].rearrange("p (m q r) -> p m q r", m=4, r=32)[:, :, :, 0],
                                       AX.X, ALU.add))
                a = PARAM_AT["b_ada"][0] + 4 * j
                dve.tensor_tensor(dst, dst, params[:, a:a + 4], ALU.add).then_inc(ada_done, 1)

            for j in range(4):
                if j == 0:
                    dve.wait_ge(in_x, 16)
                if j < TT:
                    norm_stats([xtmp[:, j, i * 512:(i + 1) * 512] for i in range(2)], j)
                ada_copy(j)
                if j == 1:
                    for t in range(TT):
                        last = normalise(xhat[:, t, :], xtmp[:, t, :], t)
                    last.then_inc(xhat_ready, 1)
                ada_finish(j)
            dve.wait_ge(ada_done, 4)
            dve.tensor_scalar(sc1p, modc[:, KD:2 * KD], 1.0, None, ALU.add).then_inc(mod1_ready, 1)
            dve.wait_ge(mod1_ready, 1)
            for j in (1, 3):
                dve.wait_ge(xt_psum, j + 1)
                for i in range(2):
                    k = 2 * j + i
                    last = dve.tensor_scalar(h_full[:, k, :], banks[j][:, i * T:(i + 1) * T], sc1p[:, k:k + 1],
                                             modc[:, k:k + 1], ALU.mult, ALU.add)
            last.then_inc(h_dve, 1)

            def split(m):
                split_by(dve, m)

            split(0)
            dve.wait_ge(h_hi_ready, 1)
            dve.tensor_tensor(h_lo, h_full, h_hi.bitcast(F32), ALU.subtract).then_inc(h_split, 1)

            split(1)
            dve.wait_ge(dt_act, 1)
            link(dve.tensor_scalar(row[7], row[0], -1.0, None, ALU.mult))
            dve.tensor_tensor(row[1], row[0], row[7], ALU.max).then_inc(dt_dve, 1)
            dve.wait_ge(dt_act, 2)
            dve.tensor_scalar(row[3], row[2], 1.0, None, ALU.add).then_inc(dt_dve, 1)
            dve.wait_ge(dt_act, 3)
            dve.wait_ge(dt_dve, 2)
            link(dve.tensor_scalar(row[5], row[3], -1.0, None, ALU.add))
            link(dve.tensor_scalar(row[7], row[5], 0.0, None, ALU.is_equal))
            dve.tensor_tensor(row[4], row[4], row[7], ALU.add)
            link(dve.tensor_tensor(row[5], row[5], row[7], ALU.add))
            link(dve.reciprocal(row[5], row[5]))
            link(dve.tensor_tensor(row[2], row[2], row[4], ALU.mult))
            link(dve.tensor_tensor(row[2], row[2], row[5], ALU.mult))
            link(dve.scalar_tensor_tensor(out=row[0], in0=row[0], scalar=0.0, in1=row[2], op0=ALU.max, op1=ALU.add))
            dve.wait_ge(zeros_done, 1)
            dve.tensor_scalar(scan[0][:, :, CPAD:CPAD + CH], row[0].rearrange("p (c s) -> p c s", c=NC),
                              stat[0:2 * HEADS, 60:61], -1.0, ALU.mult, ALU.mult).then_inc(scan_in, 1)

            def conv(p):
                dve.wait_ge(conv_first, p + 1)
                m0, n0 = tile_of(p), N_STEPS * p
                for k in range(1, TAPS):
                    for i in range(2):
                        if k > 1:
                            dve.wait_ge(conv_steps, n0 + 2 * (k - 1) + i - 1)
                        dst = conv_dst(p)[:, i, :]
                        dve.scalar_tensor_tensor(out=dst, in0=stage[p % 3][:, i, k:k + T],
                                                 scalar=conv_w[:, m0 + i, k:k + 1], in1=dst, op0=ALU.mult,
                                                 op1=ALU.add).then_inc(conv_steps, 1)

            for p in range(N_CONV):
                j = (p - PAIR_OF["x"]) // 2
                if p % 2 == 0 and j >= 1:
                    ada_finish(3 + j)
                split(p + 2)
                if p % 2 and j >= 0:
                    ada_copy(4 + j)
                conv(p)
                if p == 7:
                    dve.wait_ge(dec_done, 1)
                    dve.wait_ge(scan_in, 1)
                    dve.tensor_tensor(row[7][0:HEADS, 0:CH], row[0][0:HEADS, 0:CH], row[5][0:HEADS, 0:CH], ALU.mult)
                    dve.tensor_tensor(row[7][HEADS:, 0:CH], row[0][HEADS:, CH:T], row[5][HEADS:, 0:CH],
                                      ALU.mult).then_inc(rows_done, 1)
                if p == 9:
                    dve.wait_ge(cols_psum, 1)
                    link(dve.tensor_copy(col, banks[5][:, 0:320].rearrange("p (a h) -> p a h", a=5)))
                    dve.tensor_scalar(ncol, col[:, 2:4, :], -1.0, None, ALU.mult).then_inc(cols_done, 1)

            def group_mask(g):
                dve.wait_ge(ssd_a, g + 1)
                dve.wait_ge(b_copied, g + 1)
                if g:
                    dve.wait_ge(scores_ready, g)
                for d, tri in enumerate((tri_f, tri_b)):
                    last = dve.tensor_tensor(cbm[:, d], banks[4][:, 0:256].rearrange("p (c l) -> p c l", c=NC),
                                             tri.unsqueeze(1).to_broadcast([P, NC, CH]), ALU.mult)
                last.then_inc(cb_masked, 1)

            def group_steps(g):
                dve.wait_ge(cexp_ready, g + 1)
                for d in range(2):
                    for r in range(HPG):
                        h = d * HEADS + g * HPG + r
                        for c in range(NC):
                            e = decay[g % 3][:, d, r, c * CH:(c + 1) * CH]
                            last = dve.tensor_scalar(e, e, ncol[:, c, h:h + 1], 0.0, ALU.add, ALU.min)
                last.then_inc(steps_ready, 1)

            def group_scores(g):
                dve.wait_ge(exp_ready, g + 1)
                dve.wait_ge(cb_masked, g + 1)
                for d in range(2):
                    e = decay[g % 3][:, d]
                    last = dve.tensor_tensor(e, e, cbm[:, d].rearrange("p c l -> p (c l)").unsqueeze(1).to_broadcast(
                        [P, HPG, T]), ALU.mult)
                last.then_inc(scores_ready, 1)

            def group_out(g):
                dve.wait_ge(y_psum, g + 1)
                for i in range(2):
                    k = 2 * g + i
                    a = PARAM_AT["d_skip"][0] + k
                    last = dve.scalar_tensor_tensor(out=xT[:, k, :], in0=xT[:, k, :], scalar=params[:, a:a + 1],
                                                    in1=banks[3][:, i * T:(i + 1) * T], op0=ALU.mult, op1=ALU.add)
                last.then_inc(y_out, 1)

            def pool_mean(o):
                w = POOL_ORDER[o]
                for i in range(2):
                    n = 2 * w + i
                    dve.wait_ge(pool_sums, 2 * o + i + 1)
                    buf = (sum(2 * (v + 1) for v in POOL_ORDER[:o]) + (i + 1) * (w + 1) - 1) % 3
                    s = psum_buf[buf][:, WMAX:WMAX + T]
                    for side, e0 in ((0, 0), (1, T - WMAX)):
                        last = dve.tensor_tensor(s[:, e0:e0 + WMAX], s[:, e0:e0 + WMAX], edge[:, w, side, :], ALU.mult)
                    link(last)
                    u = uT[:, n, WMAX:WMAX + T]
                    dve.scalar_tensor_tensor(out=u, in0=s, scalar=1.0 / WINDOWS[w], in1=u, op0=ALU.mult,
                                             op1=ALU.subtract).then_inc(pool_diff, 1)

            def gate_y(i):
                dve.wait_ge(y_out, 2 * i + 2)
                dve.wait_ge(z_silu, i + 1)
                dve.tensor_tensor(zT[:, 4 * i:4 * i + 4, :], xT[:, 4 * i:4 * i + 4, :], zT[:, 4 * i:4 * i + 4, :],
                                  ALU.mult).then_inc(yg_ready, 1)

            for j in range(10):
                if j <= 4:
                    ada_finish(7 + j)
                if j < 4:
                    ada_copy(8 + j)
                if j == 5:
                    dve.wait_ge(ada_done, 12)
                    link(dve.tensor_scalar(sc2p, modc[:, 4 * KD:5 * KD], 1.0, None, ALU.add))
                split(N_CONV + 2 * j + 2)
                if 1 <= j <= GROUPS:
                    group_scores(j - 1)
                if j < GROUPS:
                    group_mask(j)
                split(N_CONV + 2 * j + 3)
                if j >= 6:
                    pool_mean(j - 6)
                if j >= 2:
                    group_out(j - 2)
                if j < GROUPS:
                    group_steps(j)
                if 5 <= j <= 7:
                    gate_y(j - 5)

            gate_y(3)
            dve.wait_ge(pair_act, MIX0)

            def gate_pool(j):
                p = POUT0 + j
                dve.wait_ge(pair_ready, p + 1)
                g = gT[:, KD + 2 * j:KD + 2 * j + 2, :]
                dve.tensor_tensor(g, banks[p % 3][:, :].rearrange("p (a t) -> p a t", a=2), g,
                                  ALU.mult).then_inc(pair_dve, 1)

            for o, w in enumerate(POOL_ORDER):
                dve.wait_ge(u_hi_ready, o + 1)
                pair_of = slice(2 * w, 2 * w + 2)
                dve.tensor_tensor(u_lo[:, pair_of, :], u_full[:, pair_of, :], u_hi[:, pair_of, :].bitcast(F32),
                                  ALU.subtract).then_inc(u_lo_ready, 1)
            dve.wait_ge(gvar_psum, 1)
            link(dve.tensor_scalar(vtmp, banks[4][:, :].rearrange("p (a t) -> p a t", a=2), 1.0 / 256, EPS, ALU.mult,
                                   ALU.add))
            dve.reciprocal(vtmp, vtmp).then_inc(gvar_sb, 1)
            gate_pool(0)
            dve.wait_ge(grstd_psum, 1)
            for k in range(NX):
                g = k // 2
                a = PARAM_AT["norm_g"][0] + k
                last = dve.scalar_tensor_tensor(out=zT[:, k, :], in0=zT[:, k, :], scalar=params[:, a:a + 1],
                                                in1=banks[(5, 6, 7, 3)[g % 4]][:, (g // 4) * T:(g // 4 + 1) * T],
                                                op0=ALU.mult, op1=ALU.mult)
                if k % 4 == 3:
                    last.then_inc(yn_ready, 1)
            for i in range(4):
                dve.wait_ge(y_hi_ready, i + 1)
                dve.tensor_tensor(y_lo[i], zT[:, 4 * i:4 * i + 4, :], y_hi[i].bitcast(F32), ALU.subtract)\
                   .then_inc(y_lo_ready, 1)
            gate_pool(1)
            split(MP + 4)
            gate_pool(2)
            split(MP + 5)
            gate_pool(3)
            for j in range(4):
                p = SOUT0 + j
                hf, r = j // 2, j % 2
                dve.wait_ge(wo_hi_ready, j + 1)
                dve.tensor_tensor(wo_lo[hf][r], w_o_slot(hf)[:, 4 * r:4 * r + 4, :], wo_hi[hf][r].bitcast(F32),
                                  ALU.subtract).then_inc(wo_lo_ready, 1)
                for m in (MP + 6 + 2 * j, MP + 7 + 2 * j):
                    if m < len(splits):
                        split(m)
                dve.wait_ge(pair_ready, p + 1)
                g = gT[:, 2 * j:2 * j + 2, :]
                dve.tensor_tensor(g, banks[p % 3][:, :].rearrange("p (a t) -> p a t", a=2), g,
                                  ALU.mult).then_inc(pair_dve, 1)
                dve.wait_ge(pair_dve, p - POUT0 + 1)
                dve.tensor_tensor(g, g, gT[:, KD + 2 * j:KD + 2 * j + 2, :], ALU.add).then_inc(mix_ready, 1)
                dve.wait_ge(mix_hi_ready, j + 1)
                dve.tensor_tensor(mix_lo[:, 2 * j:2 * j + 2, :], g, mix_hi[:, 2 * j:2 * j + 2, :].bitcast(F32),
                                  ALU.subtract).then_inc(mix_lo_ready, 1)

            dve.tensor_scalar(alpha_ident, ident, ALPHA, None, ALU.mult).then_inc(alpha_ident_ready, 1)
            dve.wait_ge(in_ln, 32)
            dve.wait_ge(in_resid, 16)
            for t in range(TT):
                for hf in range(2):
                    p, cs = WO0 + 2 * t + hf, slice(hf * 512, (hf + 1) * 512)
                    dve.wait_ge(pair_ready, p + 1)
                    dve.tensor_tensor(tmp_row[:, cs], banks[p % 3][:, :], grow[:, 0, cs], ALU.mult)\
                       .then_inc(pair_dve, 1)
                    dve.wait_ge(pair_dve, p - POUT0 + 1)
                    link(dve.scalar_tensor_tensor(out=x1[:, t, cs], in0=x1[:, t, cs], scalar=ALPHA, in1=tmp_row[:, cs],
                                                  op0=ALU.mult, op1=ALU.add))
                norm_stats([x1[:, t, 0:512], x1[:, t, 512:D]], 2 + 2 * t)
                link(centre_scale(x1[:, t, :], x1[:, t, :], ln_g, 2 + 2 * t))
                ins = scale_shift(x1[:, t, :], ln_b, 2 + 2 * t)
                if t == TT - 1:
                    ins.then_inc(ln_gb_used, 1)
                    dve.wait_ge(ln_gb_used, 1)
                else:
                    link(ins)
                norm_stats([x1[:, t, 0:512], x1[:, t, 512:D]], 3 + 2 * t)
                normalise(xh2[:, t, :], x1[:, t, :], 3 + 2 * t).then_inc(xh2_ready, 1)
            dve.wait_ge(h2_psum, 2 * TT)
            t = TT - 1
            for k in range(KD // 2, KD):
                last = dve.tensor_scalar(h2T[:, k, t * P:(t + 1) * P], banks[5 + 2 * t][:, (k - 4) * P:(k - 3) * P],
                                         sc2p[:, k:k + 1], modc[:, 3 * KD + k:3 * KD + k + 1], ALU.mult, ALU.add)
            last.then_inc(h2_dve, 1)

            def small(a, n, *dims):
                v = r_t[:, a:a + TT * n]
                return v.rearrange("p (t n) -> p t n", t=TT) if not dims else \
                    v.rearrange("p (t g e) -> p t g e", t=TT, g=dims[0])

            def over(v, n):
                return v.to_broadcast([P, TT, n])

            dve.wait_ge(in_wr, 48)
            dve.wait_ge(lg_psum, TT)
            for t in range(TT):
                last = dve.tensor_tensor(lg[:, t, :], banks[4][:, t * 64:t * 64 + EG + NE], r_bias, ALU.add)
            link(last)
            g_lg = lg[:, :, 0:EG]
            e_lg = lg[:, :, EG:].rearrange("p t (g e) -> p t g e", g=EG)
            g_max, g_sum, g_w = small(20, 1), small(22, 1), small(24, 1)
            g_d, g_exp = small(0, EG), small(8, EG)
            link(dve.tensor_reduce(g_max, g_lg, AX.X, ALU.max))
            dve.tensor_tensor(g_d, g_lg, over(g_max, EG), ALU.subtract).then_inc(rt_dve, 1)

            def first_max(onehot, values, maximum, tie, tie_max, rev, n):
                link(dve.tensor_tensor(tie, values, over(maximum, n), ALU.is_equal))
                link(dve.tensor_tensor(tie, tie, rev.unsqueeze(1).to_broadcast([P, TT, n]), ALU.mult))
                link(dve.tensor_reduce(tie_max, tie, AX.X, ALU.max))
                link(dve.tensor_tensor(onehot, tie, over(tie_max, n), ALU.is_equal))

            g_hot = small(40, EG)
            first_max(g_hot, g_lg, g_max, small(32, EG), small(26, 1), const("rev4"), EG)
            picked = small(192, NE, EG)
            e_in, e_in2 = small(48, EPG), small(104, EPG)
            link(dve.tensor_tensor(picked, e_lg, g_hot.unsqueeze(3).to_broadcast([P, TT, EG, EPG]), ALU.mult))
            link(dve.tensor_reduce(e_in, picked.rearrange("p t g e -> p t e g"), AX.X, ALU.add))
            m1, m2, hot1, hot2, tie = small(64, 1), small(68, 1), small(88, EPG), small(120, EPG), small(72, EPG)
            link(dve.tensor_reduce(m1, e_in, AX.X, ALU.max))
            first_max(hot1, e_in, m1, tie, small(66, 1), const("rev8"), EPG)
            link(dve.scalar_tensor_tensor(out=e_in2, in0=hot1, scalar=-BIG, in1=e_in, op0=ALU.mult, op1=ALU.add))
            link(dve.tensor_reduce(m2, e_in2, AX.X, ALU.max))
            dve.tensor_tensor(small(16, 1), m2, m1, ALU.subtract).then_inc(rt_dve, 1)
            first_max(hot2, e_in2, m2, tie, small(66, 1), const("rev8"), EPG)
            dve.wait_ge(rt_act, 1)
            link(dve.tensor_reduce(g_sum, g_exp, AX.X, ALU.add))
            link(dve.reciprocal(g_w, g_sum))
            dve.wait_ge(rt_act, 2)
            den, w1, w2 = small(28, 1), small(30, 1), small(70, 1)
            link(dve.tensor_scalar(den, small(18, 1), 1.0, None, ALU.add))
            link(dve.reciprocal(den, den))
            link(dve.tensor_tensor(w1, den, g_w, ALU.mult))
            link(dve.tensor_tensor(w2, w1, small(18, 1), ALU.mult))
            ew, ew2, ehot = small(136, EPG), small(152, EPG), small(168, EPG)
            dve.tensor_tensor(ew, hot1, over(w1, EPG), ALU.mult)
            dve.tensor_tensor(ehot, hot1, hot2, ALU.add)
            link(dve.tensor_tensor(ew2, hot2, over(w2, EPG), ALU.mult))
            link(dve.tensor_tensor(ew, ew, ew2, ALU.add))
            g_hot4 = g_hot.unsqueeze(3).to_broadcast([P, TT, EG, EPG])
            dve.tensor_tensor(comb.rearrange("p t (g e) -> p t g e", g=EG), g_hot4,
                              ew.unsqueeze(2).to_broadcast([P, TT, EG, EPG]), ALU.mult)
            dve.tensor_tensor(msk.rearrange("p t (g e) -> p t g e", g=EG), g_hot4,
                              ehot.unsqueeze(2).to_broadcast([P, TT, EG, EPG]), ALU.mult).then_inc(mask_ready, 1)
            dve.wait_ge(mask_ready, 1)
            unrouted = small(192, NE)
            link(dve.tensor_scalar(unrouted, msk, -1.0, 1000.0, ALU.add, ALU.mult))
            dve.wait_ge(rank_psum, 1)
            dve.tensor_tensor(rk, banks[5][:, 0:2 * NE].rearrange("p (t e) -> p t e", t=TT), unrouted,
                              ALU.add).then_inc(rank_ready, 1)

            def select(it, q0):
                if q0 >= 2:
                    dve.wait_ge(gather_half, 8 * it + 2 * q0 - 2)
                    dve.wait_ge(sel_weighted, 4 * it + q0 - 1)
                dve.tensor_tensor(sel[q0 % 2].rearrange("p t (e j) -> p t e j", e=2),
                                  slot_no[:, 0:C].unsqueeze(1).unsqueeze(1).to_broadcast([P, TT, 2, C]),
                                  rk[:, :, bass.ds(8 * it + 2 * q0, 2)].unsqueeze(3).to_broadcast([P, TT, 2, C]),
                                  ALU.is_equal).then_inc(sel_ready, 1)

            dve.wait_ge(rank_ready, 1)
            select(0, 0)
            select(0, 1)
            dve.wait_ge(counts_psum, 1)
            most, over1, over2, over3 = (r_t[:, i:i + 1] for i in (400, 401, 402, 403))
            link(dve.tensor_reduce(most, banks[6][:, 0:NE], AX.X, ALU.max))
            link(dve.tensor_scalar(over1, most, float(C), 1.0, ALU.is_gt, ALU.add))
            link(dve.scalar_tensor_tensor(out=over2, in0=most, scalar=float(2 * C), in1=over1, op0=ALU.is_gt,
                                          op1=ALU.add))
            link(dve.scalar_tensor_tensor(out=over3, in0=most, scalar=float(3 * C), in1=over2, op0=ALU.is_gt,
                                          op1=ALU.add))
            dve.tensor_copy(passes_i, over3).then_inc(passes_ready, 1)

            def pair(it, q0):
                q, b = 4 * it + q0, q0 % 2
                dve.wait_ge(up_psum, q + 1)
                dve.wait_ge(hs_ready, q + 1)
                if q0:
                    dve.wait_ge(hT_psum, q)
                dve.tensor_tensor(hm, banks[7][:, :], hs, ALU.mult).then_inc(hm_ready, 1)
                dve.wait_ge(hT_psum, q + 1)
                if q0:
                    dve.wait_ge(yd_psum, 2 * q)
                dve.tensor_copy(hTs, banks[7][:, :].rearrange("p (k n) -> p k n", k=KH)).then_inc(hT_sb, 1)
                dve.wait_ge(selT_psum, q + 1)
                if q0 >= 2:
                    dve.wait_ge(scattered, q - 1)
                dve.tensor_copy(selT[b], banks[6][:, 0:T]).then_inc(selT_sb, 1)
                for n, done in enumerate((y0_sb, y1_sb)):
                    dve.wait_ge(yd_psum, 2 * q + n + 1)
                    dve.tensor_tensor(ysb[b][:, n, :], banks[6 + n][:, :], grow[:, 1, n * 512:(n + 1) * 512],
                                      ALU.mult).then_inc(done, 1)
                if q0 < NPAIR - 2:
                    select(it, q0 + 2)

            all_pairs(dve, pair)
            dve.wait_ge(scattered, NPAIR)

            def further(b, q, n):
                dve.wait_ge(more_free, n + 1)
                dve.tensor_tensor(sel[0].rearrange("p t (e j) -> p t e j", e=2),
                                  slot_no[:, bass.ds(b * C, C)].unsqueeze(1).unsqueeze(1).to_broadcast([P, TT, 2, C]),
                                  rk[:, :, bass.ds(2 * q, 2)].unsqueeze(3).to_broadcast([P, TT, 2, C]),
                                  ALU.is_equal).then_inc(more_sel, 1)
                dve.wait_ge(more_sel, 2 * n + 1)
                dve.tensor_tensor(selw[0].rearrange("p t (e j) -> p t e j", e=2),
                                  sel[0].rearrange("p t (e j) -> p t e j", e=2),
                                  comb[:, :, bass.ds(2 * q, 2)].unsqueeze(3).to_broadcast([P, TT, 2, C]),
                                  ALU.mult).then_inc(more_sel, 1)
                dve.wait_ge(more_hs, n + 1)
                dve.tensor_tensor(hm, banks[7][:, :], hs, ALU.mult).then_inc(more_hm, 1)
                dve.wait_ge(more_turned, n + 1)
                dve.tensor_copy(selT[0], banks[5][:, 0:T])
                dve.tensor_copy(hTs, banks[4][:, :].rearrange("p (k n) -> p k n", k=KH)).then_inc(more_turned_sb, 1)
                dve.wait_ge(more_down, n + 1)
                for half in range(2):
                    last = dve.tensor_tensor(ysb[0][:, half, :], banks[6 + half][:, :],
                                             grow[:, 1, half * 512:(half + 1) * 512], ALU.mult)
                last.then_inc(more_ysb, 1)
                dve.wait_ge(more_free, n + 2)

            further_passes(dve, further)
            dve.wait_ge(in_ln, 64)
            dve.wait_ge(x1_used, TT)
            for t in range(TT):
                norm_stats([banks[2 * t][:, :], banks[2 * t + 1][:, :]], 6 + t)
                for n in range(2):
                    cs = slice(n * 512, (n + 1) * 512)
                    last = centre_scale(x1[:, t, cs], banks[2 * t + n][:, :], ln_g[:, cs], 6 + t)
                link(last)
                for n in range(2):
                    cs = slice(n * 512, (n + 1) * 512)
                    scale_shift(x1[:, t, cs], ln_b[:, cs], 6 + t).then_inc(out_ready, 1)


def shape_constants():
    a = {}
    i = np.arange(P)
    a["ident"] = np.eye(P)
    a["tri_f"] = i[:, None] <= i[None, :]
    a["tri_b"] = i[:, None] >= i[None, :]
    a["strict"] = i[:, None] < i[None, :]
    a["ones"] = np.ones((P, P))
    a["every32"] = np.repeat(i[:, None] % 32 == 0, P, 1)
    a["slot"] = np.repeat(np.arange(PASSES * C)[None], P, 0)
    a["rev4"] = np.repeat(np.arange(EG, 0, -1)[None], P, 0)
    a["rev8"] = np.repeat(np.arange(EPG, 0, -1)[None], P, 0)
    t = np.arange(T)
    edge = np.stack([w / (np.minimum(t + w // 2, T) - np.maximum(t - w // 2, 0)) for w in WINDOWS])
    edge = np.stack([edge[:, :WMAX], edge[:, T - WMAX:]], 1).reshape(1, -1)
    a["edge"] = np.repeat(edge, P, 0)
    return np.concatenate([np.asarray(a[k], np.float32) for k in CONST_COLS], 1)


def packed_parameters(inp):
    def cols(v):
        return v.reshape(-1, P).T

    def rows(f, b):
        out = np.zeros((P, 1), np.float32)
        out[0:HEADS, 0], out[HEADS:2 * HEADS, 0] = f, b
        return out

    a = {
        "conv_w": inp["conv_w"][0].reshape(TAPS, 32, P).transpose(2, 1, 0).reshape(P, -1),
        "conv_b": cols(inp["conv_b"][0]), "norm_g": cols(inp["ssd_norm_g"][0]),
        "pool_scale": cols(inp["pool_scale"][0]), "gate_b": cols(inp["gate_b"][0]), "b_ada": cols(inp["b_ada"][0]),
        "d_skip": cols(np.repeat(inp["d_skip"][0], HD)), "c": cols(inp["c"][0]),
        "dt_bias": rows(inp["dt_bias_f"][0], inp["dt_bias_b"][0]), "a_log": rows(inp["a_log_f"][0], inp["a_log_b"][0]),
    }
    return np.concatenate([a[k] for k in PARAM_COLS], 1)


STREAMED = ["x", "w_ada", "b_ada", "w_in", "pool_w", "w_pool_out", "w_ssd_out", "w_o", "ln1_g", "ln1_b", "router_wg",
            "router_we", "exp_w_gate", "exp_w_up", "exp_w_down", "ln2_g", "ln2_b"]


def kernel(**inputs):
    import concourse.bacc as bacc
    from concourse.bass_utils import run_bass_kernel_spmd

    inp = {k: np.ascontiguousarray(v) for k, v in inputs.items()}
    nc = bacc.Bacc("TRN2", target_bir_lowering=False, num_devices=1)
    arrays = {k: inp[k] for k in STREAMED}
    arrays["consts"] = shape_constants()
    arrays["params"] = packed_parameters(inp)
    arrays["router_b"] = np.concatenate([inp["router_bg"], inp["router_be"]], 1)
    t = {k: nc.dram_tensor(f"in_{k}", a.shape, F32, kind="ExternalInput").ap() for k, a in arrays.items()}
    out = nc.dram_tensor("out", inp["x"].shape, F32, kind="ExternalOutput").ap()
    build(nc, t, t["consts"], t["params"], t["router_b"], out)
    r = run_bass_kernel_spmd(nc, [{f"in_{k}": a for k, a in arrays.items()}], core_ids=[0])
    return r.results[0]["out"]
```
